# Optimizing a Trainium2 kernel written in Bass

```python
import jax, jax.numpy as jnp
from jax import lax
import numpy as np

D_MODEL = 1024
BATCH = 1
SEQ = 256
DEPTH = 2

N_MIXERS = 4
ALPHA = (2 * DEPTH) ** 0.25
BETA = (8 * DEPTH) ** -0.25
LN_EPS = 1e-5

SHORT_CONV_WIDTH = 3

CHUNK = 128
GMLP_FFN = 6 * D_MODEL
GMLP_HALF = GMLP_FFN // 2
GMLP_HEADS = 8

POOL_WINDOWS = (2, 4, 8, 16)
POOL_GROUPS = len(POOL_WINDOWS)
POOL_GW = D_MODEL // POOL_GROUPS

CONF_CONV_WIDTH = 31

N_EXPERTS = 64
TOP_K = 8
N_EXPERT_GROUPS = 8
TOPK_GROUPS = 4
EXPERT_HIDDEN = 256
SHARED_HIDDEN = 256
ROUTED_SCALE = 2.5
MOE_BLOCK = 128

kernel_name = "hybrid_conv_gmlp_pool_conformer_moe"

def layer_norm(x, g, b):
    xf = x.astype(jnp.float32)
    mu = jnp.mean(xf, axis=-1, keepdims=True)
    var = jnp.mean(jnp.square(xf - mu), axis=-1, keepdims=True)
    return ((xf - mu) * lax.rsqrt(var + LN_EPS) * g + b).astype(x.dtype)

def causal_depthwise_conv(x, w):
    width, ch = w.shape
    return lax.conv_general_dilated(
        x, w[:, None, :].astype(x.dtype), window_strides=(1,), padding=[(width - 1, 0)],
        dimension_numbers=("NWC", "WIO", "NWC"), feature_group_count=ch)

def gated_short_conv(x, w_in, conv_w, w_out):
    b_gate, c_gate, xt = jnp.split(x @ w_in, 3, axis=-1)
    y = b_gate * causal_depthwise_conv(c_gate * xt, conv_w)
    return y @ w_out

def chunked_spatial_gating(x, w_in, v_ln_g, v_ln_b, w_s, s_bias, w_out):
    bsz, seq, _ = x.shape
    u, v = jnp.split(jax.nn.gelu(x @ w_in), 2, axis=-1)
    v = layer_norm(v, v_ln_g, v_ln_b)
    v = v.reshape(bsz, seq // CHUNK, CHUNK, GMLP_HEADS, GMLP_HALF // GMLP_HEADS)
    w_causal = jnp.tril(w_s)
    s = jnp.einsum("hts,bcshd->bcthd", w_causal, v) + s_bias.T[:, :, None]
    return (u * s.reshape(bsz, seq, GMLP_HALF)) @ w_out

def multiscale_pool(x, w_in, w_grp, scale, w_out):
    bsz, seq, d = x.shape
    h = x @ w_in
    csum = jnp.cumsum(h.astype(jnp.float32), axis=1)
    pos = jnp.arange(1, seq + 1, dtype=jnp.float32)
    outs = []
    for g, win in enumerate(POOL_WINDOWS):
        c = csum[..., g * POOL_GW:(g + 1) * POOL_GW]
        lag = jnp.pad(c, ((0, 0), (win, 0), (0, 0)))[:, :seq]
        mean = (c - lag) / jnp.minimum(pos, float(win))[None, :, None]
        outs.append(mean.astype(h.dtype) - h[..., g * POOL_GW:(g + 1) * POOL_GW])
    p = jnp.stack(outs, axis=2)
    y = jnp.einsum("btgc,gce->btge", p, w_grp).reshape(bsz, seq, d) * scale
    return y @ w_out

def conformer_conv(x, w_in, conv_w, conv_b, ln_g, ln_b, w_out):
    a, gate = jnp.split(x @ w_in, 2, axis=-1)
    h = a * jax.nn.sigmoid(gate)
    h = causal_depthwise_conv(h, conv_w) + conv_b
    h = jax.nn.silu(layer_norm(h, ln_g, ln_b))
    return h @ w_out

def moe(x, router_w, router_bias, w_gate, w_up, w_down, sh_gate, sh_up, sh_down):
    bsz, seq, d = x.shape
    xt = x.reshape(-1, d)
    n_tok = xt.shape[0]
    scores = jax.nn.sigmoid((xt @ router_w).astype(jnp.float32))
    biased = scores + router_bias.astype(jnp.float32)
    per_grp = N_EXPERTS // N_EXPERT_GROUPS
    grp_score = lax.top_k(biased.reshape(n_tok, N_EXPERT_GROUPS, per_grp), 2)[0].sum(-1)
    _, top_grp = lax.top_k(grp_score, TOPK_GROUPS)
    grp_mask = jax.nn.one_hot(top_grp, N_EXPERT_GROUPS).sum(1) > 0
    masked = jnp.where(jnp.repeat(grp_mask, per_grp, axis=1), biased, -jnp.inf)
    _, top_e = lax.top_k(masked, TOP_K)
    gate = jnp.take_along_axis(scores, top_e, axis=1)
    gate = gate / jnp.sum(gate, axis=-1, keepdims=True) * ROUTED_SCALE

    n_assign = n_tok * TOP_K
    flat_e = top_e.reshape(-1)
    flat_tok = jnp.broadcast_to(jnp.arange(n_tok, dtype=jnp.int32)[:, None], (n_tok, TOP_K)).reshape(-1)
    flat_w = gate.reshape(-1).astype(x.dtype)
    order = jnp.argsort(flat_e)
    se, st, sw = flat_e[order], flat_tok[order], flat_w[order]
    counts = jnp.bincount(flat_e, length=N_EXPERTS)
    padded = (counts + MOE_BLOCK - 1) // MOE_BLOCK * MOE_BLOCK
    pad_end = jnp.cumsum(padded)
    pad_start = pad_end - padded
    start = jnp.cumsum(counts) - counts
    dest = pad_start[se] + jnp.arange(n_assign) - start[se]
    n_blocks = (n_assign + N_EXPERTS * (MOE_BLOCK - 1) + MOE_BLOCK - 1) // MOE_BLOCK
    n_rows = n_blocks * MOE_BLOCK
    row_tok = jnp.full((n_rows,), n_tok, jnp.int32).at[dest].set(st)
    row_w = jnp.zeros((n_rows,), x.dtype).at[dest].set(sw)
    block_e = jnp.minimum(
        jnp.searchsorted(pad_end, jnp.arange(n_blocks) * MOE_BLOCK, side="right"), N_EXPERTS - 1)
    x_pad = jnp.concatenate([xt, jnp.zeros((1, d), xt.dtype)], axis=0)

    def run_block(args):
        tok, e, wt = args
        h = x_pad[tok]
        y = (jax.nn.silu(h @ w_gate[e]) * (h @ w_up[e])) @ w_down[e]
        return y * wt[:, None]

    y = lax.map(run_block, (row_tok.reshape(n_blocks, MOE_BLOCK), block_e,
                            row_w.reshape(n_blocks, MOE_BLOCK)))
    routed = jax.ops.segment_sum(y.reshape(n_rows, d), row_tok, num_segments=n_tok + 1)[:n_tok]
    shared = (jax.nn.silu(xt @ sh_gate) * (xt @ sh_up)) @ sh_down
    return (routed + shared).reshape(bsz, seq, d)

def setup_inputs(seed: int = 0) -> dict:
    key = jax.random.key(seed)
    ks = iter(jax.random.split(key, 48))

    def nrm(shape, scale):
        return jax.random.normal(next(ks), shape, jnp.float32) * scale

    def gain(shape):
        return 1.0 + 0.05 * jax.random.normal(next(ks), shape, jnp.float32)

    def bias(shape):
        return 0.02 * jax.random.normal(next(ks), shape, jnp.float32)

    n_a, n_b, n_c, n_d = (len(range(m, DEPTH, N_MIXERS)) for m in range(N_MIXERS))
    D = D_MODEL
    return {
        "x": nrm((BATCH, SEQ, D), 1.0),
        "a_w_in": nrm((n_a, D, 3 * D), D ** -0.5),
        "a_conv_w": nrm((n_a, SHORT_CONV_WIDTH, D), SHORT_CONV_WIDTH ** -0.5),
        "a_w_out": nrm((n_a, D, D), BETA * D ** -0.5),
        "b_w_in": nrm((n_b, D, GMLP_FFN), D ** -0.5),
        "b_v_ln_g": gain((n_b, GMLP_HALF)),
        "b_v_ln_b": bias((n_b, GMLP_HALF)),
        "b_w_s": nrm((n_b, GMLP_HEADS, CHUNK, CHUNK), CHUNK ** -0.5),
        "b_s_bias": gain((n_b, GMLP_HEADS, CHUNK)),
        "b_w_out": nrm((n_b, GMLP_HALF, D), BETA * GMLP_HALF ** -0.5),
        "c_w_in": nrm((n_c, D, D), D ** -0.5),
        "c_w_grp": nrm((n_c, POOL_GROUPS, POOL_GW, POOL_GW), POOL_GW ** -0.5),
        "c_scale": gain((n_c, D)),
        "c_w_out": nrm((n_c, D, D), BETA * D ** -0.5),
        "d_w_in": nrm((n_d, D, 2 * D), D ** -0.5),
        "d_conv_w": nrm((n_d, CONF_CONV_WIDTH, D), CONF_CONV_WIDTH ** -0.5),
        "d_conv_b": bias((n_d, D)),
        "d_ln_g": gain((n_d, D)),
        "d_ln_b": bias((n_d, D)),
        "d_w_out": nrm((n_d, D, D), BETA * D ** -0.5),
        "ln1_g": gain((DEPTH, D)),
        "ln1_b": bias((DEPTH, D)),
        "ln2_g": gain((DEPTH, D)),
        "ln2_b": bias((DEPTH, D)),
        "router_w": nrm((DEPTH, D, N_EXPERTS), D ** -0.5),
        "router_bias": nrm((DEPTH, N_EXPERTS), 0.01),
        "exp_w_gate": nrm((DEPTH, N_EXPERTS, D, EXPERT_HIDDEN), D ** -0.5),
        "exp_w_up": nrm((DEPTH, N_EXPERTS, D, EXPERT_HIDDEN), D ** -0.5),
        "exp_w_down": nrm((DEPTH, N_EXPERTS, EXPERT_HIDDEN, D), BETA * EXPERT_HIDDEN ** -0.5),
        "sh_w_gate": nrm((DEPTH, D, SHARED_HIDDEN), D ** -0.5),
        "sh_w_up": nrm((DEPTH, D, SHARED_HIDDEN), D ** -0.5),
        "sh_w_down": nrm((DEPTH, SHARED_HIDDEN, D), BETA * SHARED_HIDDEN ** -0.5),
    }

def reference(x, a_w_in, a_conv_w, a_w_out,
              b_w_in, b_v_ln_g, b_v_ln_b, b_w_s, b_s_bias, b_w_out,
              c_w_in, c_w_grp, c_scale, c_w_out,
              d_w_in, d_conv_w, d_conv_b, d_ln_g, d_ln_b, d_w_out,
              ln1_g, ln1_b, ln2_g, ln2_b,
              router_w, router_bias, exp_w_gate, exp_w_up, exp_w_down,
              sh_w_gate, sh_w_up, sh_w_down):
    for i in range(DEPTH):
        m, j = i % N_MIXERS, i // N_MIXERS
        if m == 0:
            h = gated_short_conv(x, a_w_in[j], a_conv_w[j], a_w_out[j])
        elif m == 1:
            h = chunked_spatial_gating(x, b_w_in[j], b_v_ln_g[j], b_v_ln_b[j], b_w_s[j],
                                       b_s_bias[j], b_w_out[j])
        elif m == 2:
            h = multiscale_pool(x, c_w_in[j], c_w_grp[j], c_scale[j], c_w_out[j])
        else:
            h = conformer_conv(x, d_w_in[j], d_conv_w[j], d_conv_b[j], d_ln_g[j], d_ln_b[j],
                               d_w_out[j])
        x = layer_norm(ALPHA * x + h, ln1_g[i], ln1_b[i])
        f = moe(x, router_w[i], router_bias[i], exp_w_gate[i], exp_w_up[i], exp_w_down[i],
                sh_w_gate[i], sh_w_up[i], sh_w_down[i])
        x = layer_norm(ALPHA * x + f, ln2_g[i], ln2_b[i])
    return x


_drawn_inputs = setup_inputs


def setup_inputs(seed=0):
    import zlib

    import numpy as np

    out = dict(_drawn_inputs(seed))
    spreads = {}
    factors = {'b_v_ln_g': 3.003, 'b_v_ln_b': 4.798, 'b_s_bias': 3.114}
    for name, (base, spread) in spreads.items():
        noise = np.random.default_rng([zlib.crc32(name.encode()), seed]).standard_normal(out[name].shape)
        drawn = base * np.exp(spread * noise) if base else spread * noise
        out[name] = __import__('jax').numpy.asarray(drawn.astype(out[name].dtype))
    for name, factor in factors.items():
        out[name] = (out[name] * factor).astype(out[name].dtype)
    return out
```

```python
from contextlib import ExitStack

import concourse.bass as bass
from concourse import mybir

FP32 = mybir.dt.float32
FP32R = mybir.dt.float32r
I32 = mybir.dt.int32
ALU = mybir.AluOpType
ACT = mybir.ActivationFunctionType
AX = mybir.AxisListType

D = 1024
T = 256
P = 128
TT = T // P
KC = D // P
DEPTH = 2
ALPHA = (2 * DEPTH) ** 0.25
LN_EPS = 1e-5
HALF = 512
GF = 3 * D
GT = GF // P
HEADS = 8
TILES_PER_HEAD = GT // HEADS
E = 64
GROUPS = 8
PER_GROUP = E // GROUPS
TOPK_GROUPS = 4
ROUTED_SCALE = 2.5
H = 256
HC = H // P
SLOTS = 64
SPAN = SLOTS
QUAD = 4
QUADS = E // QUAD
PASSES = T // SLOTS
RING = 4
SLOT = 3 * D * H // P
GU = 2 * D * H // P
NEG = -1e30

FILLS = [
    [("a_in", j) for j in range(4)] + [("a_out", 0), ("a_out", 1), ("shared", 0)],
    [("b_in", j) for j in range(8)] + [("b_out", j) for j in range(4)] + [("shared", 1)],
]
FIRST_FILL = [0, len(FILLS[0])]
EXPERT_SLOT = [len(FILLS[0]) % RING, (len(FILLS[0]) + len(FILLS[1])) % RING]
FILL_DMAS = {"a_in": 3, "a_out": 1, "b_in": 1, "b_out": 1, "shared": 3}
ALL_FILLS = FILLS[0] + FILLS[1]


class Named(dict):

    def __getattr__(self, name):
        return self[name]


def fill_ready(n):
    return 16 * sum(FILL_DMAS[ALL_FILLS[m][0]] for m in range(n % RING, n + 1, RING))


def run_totals(n):
    totals = {"s_ready": n + 1, "gathered": 4 * n + 4, "info_done": n + 1, "xs_ready": 4 * n + 4,
              "info_taken": n + 1, "y_done": 4 * n, "yh_ready": 4 * n, "yl_ready": 4 * n + 4,
              "c_ready": n + 1, "comb_done": 4 * n + 4, "comb_taken": 4 * n + 6}
    totals |= {name: 2 * n for name in ("gu_done", "sig_ready", "gated", "h_ready", "hT_done", "hT_ready")}
    totals |= {f"gu{s}": 32 * n for s in range(RING)}
    totals |= {f"dn{s}": 16 * n for s in range(RING)}
    return totals


def fills_before(n):
    return n // RING


def build(nc, x, xT0, a_w_in, a_conv_w, a_w_out, b_w_in, b_ln, b_wsT, b_w_out, rows, router_w,
          router_bias, w_gate, w_up, w_down, sh_gate, sh_up, sh_down, out):
    ctx = ExitStack()
    with ctx:
        place = [(nc.sbuf_base + 63) // 64 * 64]

        def sb(name, shape, dt=FP32):
            t = nc.alloc_sbuf_tensor_at(name, shape, dt, offset=place[0])
            words = 1
            for n in shape[1:]:
                words *= n
            place[0] += (4 * words + 63) // 64 * 64
            return t

        def sems(prefix, names):
            return Named({n: ctx.enter_context(nc.semaphore(f"{prefix}_{n}")) for n in names.split()})

        ring = sb("ring", [P, RING, SLOT])
        x_tok = sb("x_tok", [P, TT, D])
        xT = sb("xT", [P, KC, T])
        acc = sb("acc", [P, TT, D])
        rw = sb("rw", [P, DEPTH, KC, E])
        rb = sb("rb", [P, DEPTH, E])
        row = sb("row", [9, D])
        ident = sb("ident", [P, P])
        ones = sb("ones", [P, P])
        before = sb("before", [P, P])
        causal = sb("causal", [P, P])
        tok_i = sb("tok_i", [P, T], I32)
        tok = sb("tok", [P, T])
        slot_i = sb("slot_i", [P, QUAD * SLOTS], I32)
        slot_no = sb("slot_no", [P, QUAD * SLOTS])
        tri_i = sb("tri_i", [P, GROUPS, GROUPS], I32)
        tri = sb("tri", [P, GROUPS, GROUPS])
        own_i = sb("own_i", [P, TT], I32)
        stats = sb("stats", [P, TT, 8, 6])
        mv = sb("mv", [P, TT, 2])
        var_eps = sb("var_eps", [P, TT])
        rstd = sb("rstd", [P, TT])
        minus_half = sb("minus_half", [P, TT])
        shared_base = place[0]
        conv_w = sb("conv_w", [P, KC, 3])
        c_gate = sb("c_gate", [P, 2, T])
        padded = sb("padded", [P, 2, T + 2])
        conv = sb("conv", [P, T])
        aT = sb("aT", [P, KC, T])
        place[0] = shared_base
        v = sb("v", [P, TT, GF])
        uT = sb("uT", [P, GT, T])
        wsT = sb("wsT", [P, HEADS, P])
        ws_sum = sb("ws_sum", [P, HEADS, P])
        s_bias = sb("s_bias", [P, HEADS, P])
        b_gb = sb("b_gb", [P, 2, GT])
        s_off = sb("s_off", [P, 2, P])
        s_val = sb("s_val", [P, 2, T])
        end_b = place[0]
        place[0] = shared_base
        xh = sb("xh", [P, TT, KC, P], FP32R)
        xl = sb("xl", [P, TT, KC, P], FP32R)
        score = sb("score", [P, TT, E])
        biased = sb("biased", [P, TT, E])
        top8 = sb("top8", [P, TT, GROUPS, 8])
        g_score = sb("g_score", [P, TT, GROUPS])
        g_more = sb("g_more", [P, TT, GROUPS, GROUPS])
        g_tied = sb("g_tied", [P, TT, GROUPS, GROUPS])
        g_rank = sb("g_rank", [P, TT, GROUPS])
        masked = sb("masked", [P, TT, E])
        best = sb("best", [P, TT, 8])
        marked = sb("marked", [P, TT, E])
        chosen = sb("chosen", [P, TT, E])
        w_sum = sb("w_sum", [P, TT])
        w_inv = sb("w_inv", [P, TT])
        gates = sb("gates", [P, TT, PASSES * E + QUAD])
        rank = sb("rank", [P, TT, PASSES * E + QUAD])
        count = sb("count", [P, 1])
        over_f = sb("over_f", [P, 1])
        over = sb("over", [1, 1], I32)
        sel = sb("sel", [P, TT, QUAD * SLOTS], FP32R)
        g_cols = sb("g_cols", [P, TT, QUAD + 1])
        slot_gate = sb("slot_gate", [P, 2])
        slot_tok = sb("slot_tok", [P, 2])
        back = sb("back", [P, 2, T], FP32R)
        xsT = sb("xsT", [P, KC, QUAD * SLOTS])
        sig = sb("sig", [P, 2, H])
        gated = sb("gated", [P, 2, H])
        hid = sb("hid", [P, 2, H])
        hidT = sb("hidT", [P, 2, HC * P])
        yh = sb("yh", [P, 2, D], FP32R)
        yl = sb("yl", [P, 2, D], FP32R)
        assert max(place[0], end_b) <= nc.sbuf_usable_end
        ps = ctx.enter_context(nc.psum_tensor("ps", [P, 8, HALF], FP32))

        g = sems("g", "xT0 x_in const small row_in ws_in iotas stored load0 load1 load2 load3 vstep")
        load = [g.load0, g.load1, g.load2, g.load3]
        L = [sems(f"l{i}", "proj c_copied a_ready mixed ln_rows ln_var ln_rstd x_ready xT_done xT_ready xh_ready "
                           "xl_ready logits scored chosen ranks over sh_gu sh_sig sh_h sh_hT sh_hT_ready sh_y "
                           "acc_ready ln2_rows ln2_var ln2_rstd x2_ready x2T_done x2T_ready") for i in range(DEPTH)]
        B = sems("b", "ws_masked sums sums_ready v_proj v_gelu v_var v_rstd v_norm u_proj u_gelu spatial y_ready")
        SECTION = ("s_ready gathered info_done xs_ready info_taken gu_done sig_ready gated h_ready hT_done hT_ready "
                   "y_done yh_ready yl_ready c_ready comb_done comb_taken gu0 gu1 gu2 gu3 dn0 dn1 dn2 dn3")
        K = sems("k", SECTION)
        RUNS, at = [], Named({n: 0 for n in SECTION.split()})
        for run in range(2 * DEPTH):
            steps = QUADS if run % 2 == 0 else QUADS * (PASSES - 1)
            k = Named(K, base=Named(at), totals=run_totals(steps), gu_load=[K.gu0, K.gu1, K.gu2, K.gu3],
                      dn_load=[K.dn0, K.dn1, K.dn2, K.dn3])
            RUNS.append(k)
            at = {n: at[n] + k.totals[n] for n in at}
        MAIN, OVER = RUNS[0::2], RUNS[1::2]

        def skip_experts(engine, k, made_here):
            for n in made_here.split():
                engine.sem_inc(K[n], k.totals[n])

        def slot_gu(s):
            return ring[:, s, 0:GU].rearrange("p (g c h) -> p c g h", g=2, c=KC)

        def slot_dn(s):
            return ring[:, s, GU:SLOT].rearrange("p (k n) -> p k n", k=HC)

        block = ctx.enter_context(nc.Block())

        @block.sync
        def _(sp):
            def load_fill(n):
                kind, j = ALL_FILLS[n]
                s, sem = n % RING, load[n % RING]
                if kind == "a_in":
                    dst = ring[:, s, :].rearrange("p (g c n) -> p g c n", g=3, c=KC)
                    src = a_w_in.rearrange("(p c) (g n) -> p g c n", c=KC, g=3)
                    for gate in range(3):
                        sp.dma_start(dst[:, gate], src[:, gate, :, j * 256:(j + 1) * 256]).then_inc(sem, 16)
                elif kind == "a_out":
                    tiles = [6, 2][j]
                    dst = ring[:, s, 0:tiles * D].rearrange("p (c n) -> p c n", c=tiles)
                    src = a_w_out.rearrange("(c p) n -> p c n", p=P)
                    sp.dma_start(dst, src[:, 6 * j:6 * j + tiles]).then_inc(sem, 16)
                elif kind == "b_in":
                    first = GF + j * 768 if j < 4 else (j - 4) * 768
                    dst = ring[:, s, :].rearrange("p (c n) -> p c n", c=KC)
                    src = b_w_in.rearrange("(p c) n -> p c n", c=KC)
                    sp.dma_start(dst, src[:, :, first:first + 768]).then_inc(sem, 16)
                elif kind == "b_out":
                    dst = ring[:, s, :].rearrange("p (c n) -> p c n", c=6)
                    src = b_w_out.rearrange("(c p) n -> p c n", p=P)
                    sp.dma_start(dst, src[:, 6 * j:6 * j + 6]).then_inc(sem, 16)
                else:
                    for lo, w, c in ((0, sh_gate, KC), (GU // 2, sh_up, KC), (GU, sh_down, HC)):
                        n_words = w.shape[1] * w.shape[2] // P
                        sp.dma_start(ring[:, s, lo:lo + n_words], w[j].rearrange("(p c) n -> p (c n)", c=c)).then_inc(sem, 16)

            def wait_used(n):
                kind, j = ALL_FILLS[n]
                if kind == "a_in":
                    sp.wait_ge(L[0].proj, 3 * 2 * (j + 1))
                elif kind == "a_out":
                    sp.wait_ge(L[0].mixed, j + 1)
                elif kind == "b_in":
                    sp.wait_ge(B.v_proj, 4 * (j + 1)) if j < 4 else sp.wait_ge(B.u_proj, 6 * (j - 3))
                elif kind == "b_out":
                    sp.wait_ge(L[1].mixed, j + 1)
                else:
                    sp.wait_ge(L[j].sh_y, TT)

            def load_expert(layer, s, expert, k, done=None, p=0):
                src = lambda w, c: w[layer, bass.ds(expert, 1)].rearrange("e (p c) n -> (e p) (c n)", c=c)
                if done is not None:
                    sp.wait_ge(k.gu_done, k.base.gu_done + (done * 2 + (p - 1)))
                sp.dma_start(ring[:, s, 0:GU // 2], src(w_gate, KC)).then_inc(k.gu_load[s], 16)
                sp.dma_start(ring[:, s, GU // 2:GU], src(w_up, KC)).then_inc(k.gu_load[s], 16)
                if done is not None:
                    sp.wait_ge(k.y_done, k.base.y_done + (done * 4 + (2 * p - 2)))
                sp.dma_start(ring[:, s, GU:SLOT], src(w_down, HC)).then_inc(k.dn_load[s], 16)

            sp.dma_start(xT[:], xT0).then_inc(g.xT0, 16)
            for layer in range(DEPTH):
                for n in range(FIRST_FILL[layer], FIRST_FILL[layer] + len(FILLS[layer])):
                    s = n % RING
                    if layer and n - FIRST_FILL[layer] < RING:
                        sp.wait_ge(MAIN[layer - 1].y_done, MAIN[layer - 1].base.y_done + (4 * (QUADS - 1) + 2 * ((s - EXPERT_SLOT[layer - 1]) % RING // 2) + 2))
                    elif fills_before(n):
                        wait_used(n - RING)
                    load_fill(n)
                k, base = MAIN[layer], EXPERT_SLOT[layer]
                total = FIRST_FILL[layer] + len(FILLS[layer])
                for j in range(QUAD):
                    s = (base + j) % RING
                    wait_used(total + j - RING)
                    if layer and j == 0:
                        with sp.If(more > 0):
                            sp.nop()
                        with sp.Else():
                            skip_experts(sp, OVER[0], "gu0 gu1 gu2 gu3 dn0 dn1 dn2 dn3")
                    load_expert(layer, s, j, k)
                with sp.Fori(1, QUADS) as i:
                    for j in range(QUAD):
                        load_expert(layer, (base + j) % RING, i * QUAD + j, k, i, j // 2)
                o = OVER[layer]
                sp.wait_ge(L[layer].over, 1)
                more = sp.value_load(over[0:1, 0:1], min_val=0, max_val=1)
                with sp.If(more > 0):
                    sp.wait_ge(k.y_done, k.base.y_done + (4 * QUADS))
                    for j in range(QUAD):
                        load_expert(layer, (base + j) % RING, j, o)
                    with sp.Fori(1, QUADS) as i:
                        for j in range(QUAD):
                            load_expert(layer, (base + j) % RING, i * QUAD + j, o, i, j // 2)
                    for again in range(2, PASSES):
                        with sp.Fori(0, QUADS) as i:
                            for j in range(QUAD):
                                done = i + (again - 1) * QUADS
                                load_expert(layer, (base + j) % RING, i * QUAD + j, o, done, j // 2)
                    sp.wait_ge(o.y_done, o.base.y_done + (4 * QUADS * (PASSES - 1)))
                    sp.nop()
                with sp.Else():
                    sp.nop()
            for t in range(TT):
                sp.wait_ge(L[DEPTH - 1].x2_ready, t + 1)
                sp.dma_start(out[t * P:(t + 1) * P, :], x_tok[:, t, :]).then_inc(g.stored, 16)
            sp.wait_ge(g.stored, 16 * TT)

        @block.gpsimd
        def _(pool):
            nc.gpsimd.memset(ones[:], 1.0).then_inc(g.const, 1)
            nc.gpsimd.memset(minus_half[:], -0.5).then_inc(g.const, 1)
            pool.wait_ge(g.const, 2)
            nc.gpsimd.affine_select(ident[:], ones[:], pattern=[[-1, P]], base=0, channel_multiplier=1,
                                    compare_op=ALU.is_equal, fill=0.0).then_inc(g.const, 1)
            nc.gpsimd.affine_select(before[:], ones[:], pattern=[[1, P]], base=0, channel_multiplier=-1,
                                    compare_op=ALU.is_gt, fill=0.0).then_inc(g.const, 1)
            nc.gpsimd.affine_select(causal[:], ones[:], pattern=[[1, P]], base=0, channel_multiplier=-1,
                                    compare_op=ALU.is_ge, fill=0.0).then_inc(g.const, 1)
            nc.gpsimd.iota(tok_i[:], [[1, T]], base=1, channel_multiplier=0).then_inc(g.iotas, 1)
            nc.gpsimd.iota(slot_i[:], [[0, QUAD], [1, SLOTS]], base=0, channel_multiplier=0).then_inc(g.iotas, 1)
            nc.gpsimd.iota(tri_i[:], [[1, GROUPS], [-1, GROUPS]], base=0, channel_multiplier=0).then_inc(g.iotas, 1)
            nc.gpsimd.iota(own_i[:], [[P, TT]], base=1, channel_multiplier=1).then_inc(g.iotas, 1)
            for layer in range(DEPTH):
                def rsqrt(var_ready, done, n=TT):
                    for t in range(n):
                        pool.wait_ge(var_ready, t + 1)
                        nc.gpsimd.tensor_tensor(rstd[:, t:t + 1], var_eps[:, t:t + 1], minus_half[:, t:t + 1],
                                                ALU.pow).then_inc(done, 1)
                if layer == 1:
                    rsqrt(B.v_var, B.v_rstd)
                rsqrt(L[layer].ln_var, L[layer].ln_rstd)
                k = MAIN[layer]
                pool.wait_ge(L[layer].x_ready, TT)
                nc.gpsimd.memset(back[:].bitcast(FP32), 0.0).then_inc(k.c_ready, 1)
                nc.gpsimd.memset(yh[:].bitcast(FP32), 0.0).then_inc(k.yl_ready, 2)
                nc.gpsimd.memset(yl[:].bitcast(FP32), 0.0).then_inc(k.yl_ready, 2)
                rsqrt(L[layer].ln2_var, L[layer].ln2_rstd)

        @block.tensor
        def _(pe):
            def transposes(ready, done, first_bank):
                for t in range(TT):
                    pe.wait_ge(ready, t + 1)
                    for c in range(KC):
                        bank = first_bank + (t * KC + c) // 4
                        last = nc.tensor.transpose(ps[:, bank, (c % 4) * P:(c % 4 + 1) * P],
                                                   x_tok[:, t, c:D:KC], ident[:])
                        if c % 4 == 3:
                            last.then_inc(done, 1)

            def ln_rows(which, layer, done):
                for j, r in enumerate((4 * layer + 2 * which, 4 * layer + 2 * which + 1)):
                    for h in range(2):
                        last = nc.tensor.matmul(ps[:, 2 * j + h, :], ident[0:9, r:r + 1].to_broadcast([9, P]),
                                                row[:, h * HALF:(h + 1) * HALF], start=True, stop=True)
                last.then_inc(done, 1)

            def gather(q, k, first, count_of):
                for cp in (first, first + 1):
                    free = count_of(4, cp - 1)
                    if free is not None:
                        pe.wait_ge(k.xs_ready, k.base.xs_ready + (free))
                    for c in (2 * cp, 2 * cp + 1):
                        dst = ps[:, 6 + cp % 2, (c % 2) * 256:(c % 2 + 1) * 256]
                        for n, (t, part) in enumerate([(t, part) for t in range(TT) for part in (xh, xl)]):
                            last = nc.tensor.matmul(dst, part[:, t, c, :], sel[:, t, :], start=(n == 0), stop=(n == 3))
                    last.then_inc(k.gathered, 1)

            def slot_info(k):
                for p in range(2):
                    for t in range(TT):
                        last = nc.tensor.matmul(ps[:, 0, 256 + 8 * p:256 + 8 * p + QUAD + 1],
                                                sel[:, t, p * P:(p + 1) * P].bitcast(FP32), g_cols[:, t, :],
                                                start=(t == 0), stop=(t == TT - 1))
                last.then_inc(k.info_done, 1)

            def combine(k, i, groups):
                for n in groups:
                    t, h = n // 2, n % 2
                    pe.wait_ge(k.comb_taken, k.base.comb_taken + (i * 4 + n + 1))
                    for p in range(2):
                        for part in (yh, yl):
                            last = nc.tensor.matmul(ps[:, 2 + n % 2, :], back[:, p, t * P:(t + 1) * P],
                                                    part[:, p, h * HALF:(h + 1) * HALF],
                                                    start=(p == 0 and part is yh), stop=(p == 1 and part is yl))
                    last.then_inc(k.comb_done, 1)

            def experts(k, base, steps):
                pe.wait_ge(k.s_ready, k.base.s_ready + (1))
                gather(0, k, 0, lambda per, off: off if off > 0 else None)
                gather(0, k, 2, lambda per, off: off if off > 0 else None)
                slot_info(k)

                def gate_up(i, p):
                    for j in (2 * p, 2 * p + 1):
                        pe.wait_ge(k.gu_load[(base + j) % RING], k.base.gu0 + (i * 32 + 32))
                    for c in range(KC):
                        for half in range(2):
                            s = (base + 2 * p + half) % RING
                            last = nc.tensor.matmul(ps[64 * half:64 * half + 64, p, :],
                                                    xsT[:, c, (2 * p + half) * SLOTS:(2 * p + half + 1) * SLOTS],
                                                    slot_gu(s)[:, c], start=(c == 0), stop=(c == KC - 1))
                    last.then_inc(k.gu_done, 1)

                def turn(i, p):
                    pe.wait_ge(k.h_ready, k.base.h_ready + (i * 2 + (p + 1)))
                    for kk in range(HC):
                        last = nc.tensor.transpose(ps[:, p, kk * P:(kk + 1) * P], hid[:, p, kk:H:HC], ident[:])
                    last.then_inc(k.hT_done, 1)

                def down(i, p):
                    pe.wait_ge(k.hT_ready, k.base.hT_ready + (i * 2 + (p + 1)))
                    for j in (2 * p, 2 * p + 1):
                        pe.wait_ge(k.dn_load[(base + j) % RING], k.base.dn0 + (i * 16 + 16))
                    for h in range(2):
                        if p == 1:
                            pe.wait_ge(k.yl_ready, k.base.yl_ready + (i * 4 + (4 + h + 1)))
                        for kk in range(HC):
                            for half in range(2):
                                s = (base + 2 * p + half) % RING
                                last = nc.tensor.matmul(ps[64 * half:64 * half + 64, 4 + h, :],
                                                        hidT[:, p, kk * P + 64 * half:kk * P + 64 * half + 64],
                                                        slot_dn(s)[:, kk, h * HALF:(h + 1) * HALF],
                                                        start=(kk == 0), stop=(kk == HC - 1))
                        last.then_inc(k.y_done, 1)

                with pe.Fori(0, steps) as i:
                    pe.wait_ge(k.xs_ready, k.base.xs_ready + (i * 4 + 4))
                    pe.wait_ge(k.info_taken, k.base.info_taken + (i + 1))
                    gate_up(i, 0)
                    pe.wait_ge(k.yl_ready, k.base.yl_ready + (i * 4 + 4))
                    pe.wait_ge(k.c_ready, k.base.c_ready + (i + 1))
                    combine(k, i, (0, 1))
                    turn(i, 0)
                    combine(k, i, (2, 3))
                    down(i, 0)
                    gate_up(i, 1)
                    pe.wait_ge(k.s_ready, k.base.s_ready + (i + 2))
                    gather(i, k, 0, lambda per, off: i * 4 + 4 + off)
                    turn(i, 1)
                    gather(i, k, 2, lambda per, off: i * 4 + 4 + off)
                    slot_info(k)
                    down(i, 1)
                pe.wait_ge(k.yl_ready, k.base.yl_ready + (steps * 4 + 4))
                pe.wait_ge(k.c_ready, k.base.c_ready + (steps + 1))
                combine(k, steps, (0, 1, 2, 3))

            pe.wait_ge(g.const, 5)
            pe.wait_ge(g.xT0, 16)
            pe.wait_ge(g.row_in, 16)
            for layer in range(DEPTH):
                W = L[layer]
                if layer == 0:
                    for dt in range(KC):
                        n = dt // 2
                        if dt % 2 == 0:
                            pe.wait_ge(load[n], fill_ready(n))
                        if dt >= 2:
                            pe.wait_ge(W.a_ready, dt - 1)
                        w = ring[:, n, :].rearrange("p (g c n) -> p g c n", g=3, c=KC)
                        for gate, bank, lo in ((1, 0, 0), (2, 0, 256), (0, 1, 0)):
                            for c in range(KC):
                                last = nc.tensor.matmul(ps[:, 2 * (dt % 2) + bank, lo:lo + T],
                                                        w[:, gate, c, (dt % 2) * P:(dt % 2 + 1) * P], xT[:, c, :],
                                                        start=(c == 0), stop=(c == KC - 1))
                            last.then_inc(W.proj, 1)
                    feature_tiles, lhs, ready = KC, aT, W.a_ready
                else:
                    pe.wait_ge(L[0].x2T_ready, 4)
                    pe.wait_ge(B.ws_masked, 1)
                    for h in range(2):
                        nc.tensor.matmul(ps[:, 4 + h, :], ones[:], wsT[:, 4 * h:4 * h + 4, :].rearrange("p a b -> p (a b)"),
                                         start=True, stop=True)
                    for h in range(2):
                        last = nc.tensor.matmul(ps[:, 6 + h, :], ident[0:9, 8:9].to_broadcast([9, P]),
                                                row[:, h * HALF:(h + 1) * HALF], start=True, stop=True)
                    last.then_inc(B.sums, 1)
                    for j in range(4):
                        n = FIRST_FILL[1] + j
                        pe.wait_ge(load[n % RING], fill_ready(n))
                        w = ring[:, n % RING, :].rearrange("p (c n) -> p c n", c=KC)
                        for m in range(4):
                            t, nh = m // 2, m % 2
                            u = 4 * j + m
                            if u >= 4:
                                pe.wait_ge(B.v_gelu, u - 3)
                            for c in range(KC):
                                last = nc.tensor.matmul(ps[:, u % 4, 0:384], xT[:, c, t * P:(t + 1) * P],
                                                        w[:, c, nh * 384:(nh + 1) * 384], start=(c == 0), stop=(c == KC - 1))
                            last.then_inc(B.v_proj, 1)
                    for f in range(GT):
                        n = FIRST_FILL[1] + 4 + f // 6
                        if f % 6 == 0:
                            pe.wait_ge(load[n % RING], fill_ready(n))
                        w = ring[:, n % RING, :].rearrange("p (c n) -> p c n", c=KC)
                        pe.wait_ge(B.v_gelu, 16) if f < 4 else pe.wait_ge(B.u_gelu, f - 3)
                        for c in range(KC):
                            last = nc.tensor.matmul(ps[:, f % 4, 0:T], w[:, c, (f % 6) * P:(f % 6 + 1) * P], xT[:, c, :],
                                                    start=(c == 0), stop=(c == KC - 1))
                        last.then_inc(B.u_proj, 1)
                    pe.wait_ge(B.u_gelu, GT)
                    pe.wait_ge(B.v_norm, TT)
                    pe.wait_ge(B.sums_ready, 2)
                    feature_tiles, lhs, ready = GT, uT, B.y_ready

                def spatial(f):
                    if f >= 4:
                        pe.wait_ge(B.y_ready, f - 3)
                    for t in range(TT):
                        last = nc.tensor.matmul(ps[:, 4 + f % 4, t * P:(t + 1) * P], v[:, t, f * P:(f + 1) * P],
                                                wsT[:, f // TILES_PER_HEAD, :], start=True, stop=True)
                    last.then_inc(B.spatial, 1)

                out_bank = 4 if layer == 0 else 0
                lead = 3
                if layer:
                    for f in range(lead):
                        spatial(f)
                first_out = 4 if layer == 0 else FIRST_FILL[1] + 8
                for f in range(feature_tiles):
                    n = first_out + f // 6
                    if f % 6 == 0:
                        pe.wait_ge(load[n % RING], fill_ready(n))
                    pe.wait_ge(ready, f + 1)
                    w = ring[:, n % RING, :].rearrange("p (c n) -> p c n", c=6)
                    for t in range(TT):
                        for h in range(2):
                            last = nc.tensor.matmul(ps[:, out_bank + 2 * t + h, :], lhs[:, f, t * P:(t + 1) * P],
                                                    w[:, f % 6, h * HALF:(h + 1) * HALF],
                                                    start=(f == 0), stop=(f == feature_tiles - 1))
                    if f % 6 == 5 or f == feature_tiles - 1:
                        last.then_inc(W.mixed, 1)
                    if layer and f + lead < GT:
                        spatial(f + lead)
                if layer:
                    pe.wait_ge(W.ln_var, TT)
                ln_rows(0, layer, W.ln_rows)
                transposes(W.x_ready, W.xT_done, 4)
                pe.wait_ge(W.xT_ready, 4)
                for t in range(TT):
                    for c in range(KC):
                        last = nc.tensor.matmul(ps[:, 0, t * E:(t + 1) * E], xT[:, c, t * P:(t + 1) * P], rw[:, layer, c, :],
                                                start=(c == 0), stop=(c == KC - 1))
                last.then_inc(W.logits, 1)
                n = FIRST_FILL[layer] + len(FILLS[layer]) - 1
                s = n % RING
                pe.wait_ge(load[s], fill_ready(n))
                for t in range(TT):
                    for c in range(KC):
                        last = nc.tensor.matmul(ps[:, 1 + t, :], xT[:, c, t * P:(t + 1) * P], slot_gu(s)[:, c],
                                                start=(c == 0), stop=(c == KC - 1))
                    last.then_inc(W.sh_gu, 1)
                pe.wait_ge(W.chosen, 1)
                nc.tensor.matmul(ps[:, 3, 0:E], before[:], chosen[:, 0, :], start=True, stop=True)
                nc.tensor.matmul(ps[:, 3, E:2 * E], ones[:], chosen[:, 0, :], start=True, stop=False)
                nc.tensor.matmul(ps[:, 3, E:2 * E], before[:], chosen[:, 1, :], start=False, stop=True)
                nc.tensor.matmul(ps[:, 3, 2 * E:3 * E], ones[:], chosen[:, 0, :], start=True, stop=False)
                nc.tensor.matmul(ps[:, 3, 2 * E:3 * E], ones[:], chosen[:, 1, :], start=False, stop=True).then_inc(W.ranks, 1)
                pe.wait_ge(W.sh_h, TT)
                for t in range(TT):
                    for kk in range(HC):
                        last = nc.tensor.transpose(ps[:, 1, kk * T + t * P:kk * T + (t + 1) * P], hid[:, t, kk:H:HC], ident[:])
                last.then_inc(W.sh_hT, 1)
                pe.wait_ge(W.sh_hT_ready, 1)
                for t in range(TT):
                    for h in range(2):
                        for kk in range(HC):
                            last = nc.tensor.matmul(ps[:, 4 + 2 * t + h, :],
                                                    gated[:].rearrange("p a b -> p (a b)")[:, kk * T + t * P:kk * T + (t + 1) * P],
                                                    slot_dn(s)[:, kk, h * HALF:(h + 1) * HALF],
                                                    start=(kk == 0), stop=(kk == HC - 1))
                    last.then_inc(W.sh_y, 1)
                pe.wait_ge(W.xl_ready, TT)
                pe.wait_ge(W.acc_ready, TT)
                experts(MAIN[layer], EXPERT_SLOT[layer], QUADS)
                pe.wait_ge(W.over, 1)
                more = pe.value_load(over[0:1, 0:1], min_val=0, max_val=1)
                k = MAIN[layer]
                pe.wait_ge(k.xs_ready, k.base.xs_ready + (4 * QUADS + 4))
                pe.wait_ge(k.info_taken, k.base.info_taken + (QUADS + 1))
                pe.wait_ge(k.comb_taken, k.base.comb_taken + (4 * QUADS + 6))
                with pe.If(more > 0):
                    experts(OVER[layer], EXPERT_SLOT[layer], QUADS * (PASSES - 1))
                    pe.wait_ge(OVER[layer].comb_taken, OVER[layer].base.comb_taken + (4 * QUADS * (PASSES - 1) + 6))
                    pe.nop()
                with pe.Else():
                    if layer == 0:
                        skip_experts(pe, OVER[layer], "gathered info_done gu_done hT_done y_done comb_done")
                    else:
                        pe.nop()
                ln_rows(1, layer, W.ln2_rows)
                if layer + 1 < DEPTH:
                    transposes(W.x2_ready, W.x2T_done, 4)

        @block.scalar
        def _(act):
            def copy_xT(done, ready):
                for n in range(4):
                    act.wait_ge(done, n + 1)
                    t, c = n // 2, 4 * (n % 2)
                    nc.scalar.copy(xT[:, c:c + 4, t * P:(t + 1) * P],
                                   ps[:, 4 + n, :].rearrange("p (c t) -> p c t", c=4)).then_inc(ready, 1)

            def experts(k, steps):
                def copy_gathered(n_done, first):
                    for cp in (first, first + 1):
                        act.wait_ge(k.gathered, k.base.gathered + (n_done + (cp + 1)))
                        nc.scalar.copy(xsT[:, 2 * cp:2 * cp + 2, :],
                                       ps[:, 6 + cp % 2, :].rearrange("p (c t) -> p c t", c=2)).then_inc(k.xs_ready, 1)

                def sigmoid(i, p):
                    act.wait_ge(k.gu_done, k.base.gu_done + (i * 2 + (p + 1)))
                    nc.scalar.activation(sig[:, p, :], ps[:, p, 0:H], ACT.Sigmoid).then_inc(k.sig_ready, 1)

                def copy_hT(i, p):
                    act.wait_ge(k.hT_done, k.base.hT_done + (i * 2 + (p + 1)))
                    nc.scalar.copy(hidT[:, p, :], ps[:, p, 0:HC * P]).then_inc(k.hT_ready, 1)

                def high_part(i, p):
                    for h in range(2):
                        act.wait_ge(k.y_done, k.base.y_done + (i * 4 + (2 * p + h + 1)))
                        nc.scalar.copy(yh[:, p, h * HALF:(h + 1) * HALF], ps[:, 4 + h, :]).then_inc(k.yh_ready, 1)

                copy_gathered(0, 0)
                copy_gathered(0, 2)
                with act.Fori(0, steps) as i:
                    sigmoid(i, 0)
                    copy_hT(i, 0)
                    high_part(i, 0)
                    sigmoid(i, 1)
                    copy_gathered(i * 4 + 4, 0)
                    copy_hT(i, 1)
                    copy_gathered(i * 4 + 4, 2)
                    high_part(i, 1)

            act.dma_start(conv_w[:], a_conv_w).then_inc(g.small, 16)
            act.dma_start(row[:], rows).then_inc(g.row_in, 16)
            act.dma_start(x_tok[:], x.rearrange("(t p) d -> p t d", p=P)).then_inc(g.x_in, 16)
            act.dma_start(rw[:], router_w.rearrange("l (p c) e -> p l c e", c=KC)).then_inc(g.small, 16)
            act.dma_start(rb[:], router_bias.unsqueeze(0).to_broadcast([P, DEPTH, E])).then_inc(g.small, 16)
            for layer in range(DEPTH):
                W = L[layer]
                if layer == 0:
                    for dt in range(KC):
                        act.wait_ge(W.proj, 3 * dt + 2)
                        if dt >= 2:
                            act.wait_ge(W.a_ready, dt - 1)
                        nc.scalar.copy(c_gate[:, dt % 2, :], ps[:, 2 * (dt % 2), 0:T]).then_inc(W.c_copied, 1)
                else:
                    act.wait_ge(L[0].x2_ready, TT)
                    act.dma_start(wsT[:], b_wsT).then_inc(g.ws_in, 16)
                    act.dma_start(b_gb[:], b_ln).then_inc(g.ws_in, 16)
                    act.wait_ge(B.sums, 1)
                    nc.scalar.copy(ws_sum[:].rearrange("p a b -> p (a b)"),
                                   ps[:, 4:6, :].rearrange("p a b -> p (a b)")).then_inc(B.sums_ready, 1)
                    nc.scalar.copy(s_bias[:].rearrange("p a b -> p (a b)"),
                                   ps[:, 6:8, :].rearrange("p a b -> p (a b)")).then_inc(B.sums_ready, 1)
                    for u in range(16):
                        j, t, nh = u // 4, (u // 2) % 2, u % 2
                        act.wait_ge(B.v_proj, u + 1)
                        lo = j * 768 + nh * 384
                        nc.scalar.activation(v[:, t, lo:lo + 384], ps[:, u % 4, 0:384],
                                             ACT.Gelu_apprx_tanh).then_inc(B.v_gelu, 1)
                    for f in range(GT):
                        act.wait_ge(B.u_proj, f + 1)
                        nc.scalar.activation(uT[:, f, :], ps[:, f % 4, 0:T], ACT.Gelu_apprx_tanh).then_inc(B.u_gelu, 1)
                copy_xT(W.xT_done, W.xT_ready)
                for t in range(TT):
                    act.wait_ge(W.x_ready, t + 1)
                    nc.scalar.copy(xh[:, t], x_tok[:, t, :].rearrange("p (q c) -> p c q", c=KC)).then_inc(W.xh_ready, 1)
                act.wait_ge(W.logits, 1)
                nc.scalar.activation(score[:].rearrange("p a b -> p (a b)"), ps[:, 0, 0:TT * E],
                                     ACT.Sigmoid).then_inc(W.scored, 1)
                for t in range(TT):
                    act.wait_ge(W.sh_gu, t + 1)
                    nc.scalar.activation(sig[:, t, :], ps[:, 1 + t, 0:H], ACT.Sigmoid).then_inc(W.sh_sig, 1)
                act.wait_ge(W.sh_hT, 1)
                nc.scalar.copy(gated[:].rearrange("p a b -> p (a b)"), ps[:, 1, :]).then_inc(W.sh_hT_ready, 1)
                experts(MAIN[layer], QUADS)
                act.wait_ge(W.over, 1)
                more = act.value_load(over[0:1, 0:1], min_val=0, max_val=1)
                with act.If(more > 0):
                    experts(OVER[layer], QUADS * (PASSES - 1))
                    act.nop()
                with act.Else():
                    if layer == 0:
                        act.wait_ge(W.ln2_rows, 1)
                        skip_experts(act, OVER[layer], "xs_ready sig_ready hT_ready yh_ready")
                    else:
                        act.nop()
                if layer + 1 < DEPTH:
                    copy_xT(W.x2T_done, W.x2T_ready)

        @block.vector
        def _(dve):
            steps_done = [0]

            def step(instruction):
                steps_done[0] += 1
                instruction.then_inc(g.vstep, 1)
                dve.wait_ge(g.vstep, steps_done[0])

            def moments(t, chunks, var_ready):
                step(nc.vector.bn_aggr(mv[:, t, :], stats[:, t, 0:chunks, :].rearrange("p a b -> p (a b)")))
                nc.vector.tensor_scalar(var_eps[:, t:t + 1], mv[:, t, 1:2], LN_EPS, None, ALU.add).then_inc(var_ready, 1)

            def layer_norm(rows_ready, var_ready, rstd_ready, x_ready):
                for t in range(TT):
                    for h in range(2):
                        step(nc.vector.bn_stats(stats[:, t, h, :], acc[:, t, h * HALF:(h + 1) * HALF]))
                    moments(t, 2, var_ready)
                dve.wait_ge(rows_ready, 1)
                for t in range(TT):
                    dve.wait_ge(rstd_ready, t + 1)
                    step(nc.vector.tensor_scalar(acc[:, t, :], acc[:, t, :], mv[:, t, 0:1], rstd[:, t:t + 1],
                                                 ALU.subtract, ALU.mult))
                    step(nc.vector.tensor_tensor(acc[:, t, :], acc[:, t, :],
                                                 ps[:, 0:2, :].rearrange("p a b -> p (a b)"), ALU.mult))
                    nc.vector.tensor_tensor(x_tok[:, t, :], acc[:, t, :],
                                            ps[:, 2:4, :].rearrange("p a b -> p (a b)"), ALU.add).then_inc(x_ready, 1)

            def select(k, q):
                for t in range(TT):
                    nc.vector.tensor_tensor(
                        sel[:, t, :].rearrange("p (e s) -> p e s", e=QUAD),
                        slot_no[:].rearrange("p (e s) -> p e s", e=QUAD),
                        rank[:, t, bass.ds(q, QUAD)].unsqueeze(2).to_broadcast([P, QUAD, SLOTS]), ALU.is_equal)
                nc.vector.tensor_copy(g_cols[:, :, 0:QUAD], gates[:, :, bass.ds(q, QUAD)]).then_inc(k.s_ready, 1)

            def take_info(k, n):
                dve.wait_ge(k.info_done, k.base.info_done + (n))
                nc.vector.tensor_copy(slot_gate[0:64, :], ps[0:64, 0, 256:268:10])
                nc.vector.tensor_copy(slot_gate[64:128, :], ps[64:128, 0, 257:268:10])
                nc.vector.tensor_copy(slot_tok[:], ps[:, 0, 260:269:8]).then_inc(k.info_taken, 1)

            def experts(k, first, steps):
                def hidden(i, p):
                    dve.wait_ge(k.sig_ready, k.base.sig_ready + (i * 2 + (p + 1)))
                    nc.vector.scalar_tensor_tensor(gated[:, p, :], sig[:, p, :], slot_gate[:, p:p + 1], ps[:, p, 0:H],
                                                   ALU.mult, ALU.mult).then_inc(k.gated, 1)
                    dve.wait_ge(k.gated, k.base.gated + (i * 2 + (p + 1)))
                    nc.vector.tensor_tensor(hid[:, p, :], gated[:, p, :], ps[:, p, H:2 * H], ALU.mult).then_inc(k.h_ready, 1)

                def low_part(i, p):
                    for h in range(2):
                        dve.wait_ge(k.yh_ready, k.base.yh_ready + (i * 4 + (2 * p + h + 1)))
                        cols = slice(h * HALF, (h + 1) * HALF)
                        nc.vector.tensor_tensor(yl[:, p, cols], ps[:, 4 + h, :], yh[:, p, cols].bitcast(FP32),
                                                ALU.subtract).then_inc(k.yl_ready, 1)

                def add_up(i):
                    for n in range(4):
                        t, h = n // 2, n % 2
                        dve.wait_ge(k.comb_done, k.base.comb_done + (i * 4 + n + 1))
                        dve.wait_ge(k.comb_taken, k.base.comb_taken + (i * 4 + n + 1))
                        cols = slice(h * HALF, (h + 1) * HALF)
                        nc.vector.tensor_tensor(acc[:, t, cols], acc[:, t, cols], ps[:, 2 + n % 2, :],
                                                ALU.add).then_inc(k.comb_taken, 1)

                take_info(k, 1)
                with dve.Fori(0, steps) as i:
                    dve.wait_ge(k.info_taken, k.base.info_taken + (i + 1))
                    hidden(i, 0)
                    add_up(i)
                    for p in range(2):
                        last = nc.vector.tensor_scalar(back[:, p, :], tok[:], slot_tok[:, p:p + 1], None, ALU.is_equal)
                    last.then_inc(k.c_ready, 1)
                    low_part(i, 0)
                    dve.wait_ge(k.info_done, k.base.info_done + (i + 1))
                    select(k, i * QUAD + (first + QUAD))
                    hidden(i, 1)
                    take_info(k, i + 2)
                    low_part(i, 1)
                add_up(steps)

            dve.wait_ge(g.iotas, 4)
            nc.vector.tensor_copy(tok[:], tok_i[:])
            nc.vector.tensor_copy(slot_no[:], slot_i[:])
            nc.vector.memset(padded[:, :, 0:2], 0.0)
            step(nc.vector.tensor_scalar(tri[:], tri_i[:], 0, None, ALU.is_gt))
            dve.wait_ge(g.small, 48)
            dve.wait_ge(g.x_in, 16)
            for layer in range(DEPTH):
                W = L[layer]
                if layer == 0:
                    for dt in range(KC):
                        b = dt % 2
                        dve.wait_ge(W.c_copied, dt + 1)
                        step(nc.vector.tensor_tensor(padded[:, b, 2:T + 2], c_gate[:, b, :], ps[:, 2 * b, T:2 * T], ALU.mult))
                        step(nc.vector.tensor_scalar(conv[:], padded[:, b, 2:T + 2], conv_w[:, dt, 2:3], None, ALU.mult))
                        for tap in (1, 0):
                            step(nc.vector.scalar_tensor_tensor(conv[:], padded[:, b, tap:T + tap], conv_w[:, dt, tap:tap + 1],
                                                                conv[:], ALU.mult, ALU.add))
                        dve.wait_ge(W.proj, 3 * dt + 3)
                        nc.vector.tensor_tensor(aT[:, dt, :], conv[:], ps[:, 2 * b + 1, 0:T], ALU.mult).then_inc(W.a_ready, 1)
                    out_bank = 4
                else:
                    dve.wait_ge(g.ws_in, 32)
                    nc.vector.tensor_tensor(wsT[:], wsT[:], causal[:].unsqueeze(1).to_broadcast([P, HEADS, P]),
                                            ALU.mult).then_inc(B.ws_masked, 1)
                    for u in range(16):
                        j, t, nh = u // 4, (u // 2) % 2, u % 2
                        dve.wait_ge(B.v_gelu, u + 1)
                        lo = j * 768 + nh * 384
                        last = nc.vector.bn_stats(stats[:, t, 2 * j + nh, :], v[:, t, lo:lo + 384])
                    step(last)
                    for t in range(TT):
                        moments(t, 8, B.v_var)
                    for t in range(TT):
                        dve.wait_ge(B.v_rstd, t + 1)
                        nc.vector.tensor_scalar(v[:, t, :], v[:, t, :], mv[:, t, 0:1], rstd[:, t:t + 1],
                                                ALU.subtract, ALU.mult).then_inc(B.v_norm, 1)
                    dve.wait_ge(B.sums_ready, 2)
                    for f in range(GT):
                        b, head = f % 2, f // TILES_PER_HEAD
                        step(nc.vector.scalar_tensor_tensor(s_off[:, b, :], ws_sum[:, head, :], b_gb[:, 1, f:f + 1],
                                                            s_bias[:, head, :], ALU.mult, ALU.add))
                        dve.wait_ge(B.spatial, f + 1)
                        step(nc.vector.scalar_tensor_tensor(
                            s_val[:, b, :].rearrange("p (t q) -> p t q", t=TT),
                            ps[:, 4 + f % 4, 0:T].rearrange("p (t q) -> p t q", t=TT), b_gb[:, 0, f:f + 1],
                            s_off[:, b, :].unsqueeze(1).to_broadcast([P, TT, P]), ALU.mult, ALU.add))
                        nc.vector.tensor_tensor(uT[:, f, :], s_val[:, b, :], uT[:, f, :], ALU.mult).then_inc(B.y_ready, 1)
                    out_bank = 0
                dve.wait_ge(W.mixed, 4 if layer else 2)
                for t in range(TT):
                    step(nc.vector.scalar_tensor_tensor(
                        acc[:, t, :], x_tok[:, t, :], ALPHA,
                        ps[:, out_bank + 2 * t:out_bank + 2 * t + 2, :].rearrange("p a b -> p (a b)"), ALU.mult, ALU.add))
                layer_norm(W.ln_rows, W.ln_var, W.ln_rstd, W.x_ready)
                for t in range(TT):
                    dve.wait_ge(W.xh_ready, t + 1)
                    nc.vector.tensor_tensor(xl[:, t], x_tok[:, t, :].rearrange("p (q c) -> p c q", c=KC),
                                            xh[:, t].bitcast(FP32), ALU.subtract).then_inc(W.xl_ready, 1)
                dve.wait_ge(W.scored, 1)
                step(nc.vector.tensor_tensor(biased[:], score[:], rb[:, layer, :].unsqueeze(1).to_broadcast([P, TT, E]), ALU.add))
                for t in range(TT):
                    for j in range(GROUPS):
                        last = nc.vector.max(top8[:, t, j, :], biased[:, t, j * PER_GROUP:(j + 1) * PER_GROUP])
                step(last)
                step(nc.vector.tensor_tensor(g_score[:], top8[:, :, :, 0], top8[:, :, :, 1], ALU.add))
                other, own = (g_score[:].unsqueeze(2).to_broadcast([P, TT, GROUPS, GROUPS]),
                              g_score[:].unsqueeze(3).to_broadcast([P, TT, GROUPS, GROUPS]))
                step(nc.vector.tensor_tensor(g_more[:], other, own, ALU.is_gt))
                step(nc.vector.tensor_tensor(g_tied[:], other, own, ALU.is_equal))
                step(nc.vector.tensor_tensor(g_tied[:], g_tied[:], tri[:].unsqueeze(1).to_broadcast([P, TT, GROUPS, GROUPS]), ALU.mult))
                step(nc.vector.tensor_tensor(g_more[:], g_more[:], g_tied[:], ALU.add))
                step(nc.vector.reduce_sum(g_rank[:], g_more[:], AX.X))
                step(nc.vector.tensor_scalar(g_rank[:], g_rank[:], TOPK_GROUPS - 0.5, NEG, ALU.is_gt, ALU.mult))
                step(nc.vector.tensor_tensor(
                    masked[:].rearrange("p t (g e) -> p t g e", g=GROUPS), biased[:].rearrange("p t (g e) -> p t g e", g=GROUPS),
                    g_rank[:].unsqueeze(3).to_broadcast([P, TT, GROUPS, PER_GROUP]), ALU.add))
                for t in range(TT):
                    step(nc.vector.max(best[:, t, :], masked[:, t, :]))
                    step(nc.vector.match_replace(marked[:, t, :], best[:, t, :], masked[:, t, :], 4 * NEG))
                nc.vector.tensor_tensor(chosen[:], marked[:], masked[:], ALU.is_lt).then_inc(W.chosen, 1)
                dve.wait_ge(W.chosen, 1)
                step(nc.vector.tensor_tensor(masked[:], score[:], chosen[:], ALU.mult))
                step(nc.vector.reduce_sum(w_sum[:], masked[:], AX.X))
                step(nc.vector.reciprocal(w_inv[:], w_sum[:]))
                nc.vector.memset(gates[:, :, PASSES * E:], 0.0)
                nc.vector.memset(rank[:, :, PASSES * E:], -1.0)
                for t in range(TT):
                    step(nc.vector.tensor_scalar(gates[:, t, 0:E], masked[:, t, :], w_inv[:, t:t + 1], ROUTED_SCALE,
                                                 ALU.mult, ALU.mult))
                for p in range(1, PASSES):
                    last = nc.vector.tensor_copy(gates[:, :, p * E:(p + 1) * E], gates[:, :, 0:E])
                step(last)
                step(nc.vector.tensor_copy(g_cols[:, :, QUAD], own_i[:]))
                dve.wait_ge(W.ranks, 1)
                step(nc.vector.scalar_tensor_tensor(marked[:], ps[:, 3, 0:TT * E].rearrange("p (t e) -> p t e", t=TT), 1.0,
                                                    chosen[:], ALU.add, ALU.mult))
                for p in range(PASSES):
                    last = nc.vector.tensor_scalar(rank[:, :, p * E:(p + 1) * E], marked[:], -1.0 - SPAN * p, None, ALU.add)
                step(last)
                step(nc.vector.reduce_max(count[:], ps[:, 3, 2 * E:3 * E], AX.X))
                step(nc.vector.tensor_scalar(over_f[:], count[:], SPAN + 0.5, None, ALU.is_gt))
                nc.vector.tensor_copy(over[:], over_f[0:1, :]).then_inc(W.over, 1)
                for t in range(TT):
                    dve.wait_ge(W.sh_sig, t + 1)
                    step(nc.vector.tensor_tensor(gated[:, t, :], sig[:, t, :], ps[:, 1 + t, 0:H], ALU.mult))
                    nc.vector.tensor_tensor(hid[:, t, :], gated[:, t, :], ps[:, 1 + t, H:2 * H], ALU.mult).then_inc(W.sh_h, 1)
                k = MAIN[layer]
                select(k, 0)
                nc.vector.memset(w_sum[:, 0:1], 0.0).then_inc(k.comb_taken, 2)
                for t in range(TT):
                    dve.wait_ge(W.sh_y, t + 1)
                    nc.vector.scalar_tensor_tensor(
                        acc[:, t, :], x_tok[:, t, :], ALPHA,
                        ps[:, 4 + 2 * t:6 + 2 * t, :].rearrange("p a b -> p (a b)"), ALU.mult, ALU.add).then_inc(W.acc_ready, 1)
                dve.wait_ge(W.acc_ready, TT)
                experts(k, 0, QUADS)
                more = dve.value_load(over[0:1, 0:1], min_val=0, max_val=1)
                with dve.If(more > 0):
                    o = OVER[layer]
                    dve.wait_ge(k.comb_taken, k.base.comb_taken + (4 * QUADS + 6))
                    dve.wait_ge(k.info_taken, k.base.info_taken + (QUADS + 1))
                    nc.vector.memset(back[:].bitcast(FP32), 0.0).then_inc(o.c_ready, 1)
                    nc.vector.memset(w_sum[:, 0:1], 0.0).then_inc(o.yl_ready, 4)
                    nc.vector.memset(w_sum[:, 1:2], 0.0).then_inc(o.comb_taken, 2)
                    select(o, E)
                    experts(o, E, QUADS * (PASSES - 1))
                    dve.wait_ge(o.comb_taken, o.base.comb_taken + (4 * QUADS * (PASSES - 1) + 6))
                    dve.nop()
                with dve.Else():
                    if layer == 0:
                        dve.wait_ge(W.ln2_rows, 1)
                        skip_experts(dve, OVER[layer], "s_ready info_taken gated h_ready yl_ready c_ready comb_taken")
                    else:
                        dve.nop()
                dve.wait_ge(k.comb_taken, k.base.comb_taken + (4 * QUADS + 6))
                layer_norm(W.ln2_rows, W.ln2_var, W.ln2_rstd, W.x2_ready)


def kernel(**inputs):
    import concourse.bacc as bacc
    import numpy as np
    from concourse.bass_utils import run_bass_kernel_spmd

    a = {k: np.asarray(v) for k, v in inputs.items()}
    x = np.ascontiguousarray(a["x"][0])
    arrays = {
        "x": x,
        "xT0": np.ascontiguousarray(x.T.reshape(P, KC, T)),
        "a_w_in": a["a_w_in"][0],
        "a_conv_w": np.ascontiguousarray(a["a_conv_w"][0].T.reshape(KC, P, 3).transpose(1, 0, 2)),
        "a_w_out": a["a_w_out"][0],
        "b_w_in": a["b_w_in"][0],
        "b_ln": np.ascontiguousarray(np.stack([a["b_v_ln_g"][0].reshape(GT, P).T, a["b_v_ln_b"][0].reshape(GT, P).T], 1)),
        "b_wsT": np.ascontiguousarray(a["b_w_s"][0].transpose(2, 0, 1)),
        "b_w_out": a["b_w_out"][0],
        "rows": np.stack([a[n][i] for i in range(DEPTH) for n in ("ln1_g", "ln1_b", "ln2_g", "ln2_b")]
                         + [a["b_s_bias"][0].reshape(D)]),
        "router_w": a["router_w"],
        "router_bias": a["router_bias"],
        "w_gate": a["exp_w_gate"],
        "w_up": a["exp_w_up"],
        "w_down": a["exp_w_down"],
        "sh_gate": a["sh_w_gate"],
        "sh_up": a["sh_w_up"],
        "sh_down": a["sh_w_down"],
    }
    nc = bacc.Bacc("TRN2", target_bir_lowering=False, num_devices=1)
    feeds, args = {}, []
    for name, value in arrays.items():
        value = np.ascontiguousarray(value)
        feeds[f"in_{name}"] = value
        args.append(nc.dram_tensor(f"in_{name}", value.shape, mybir.dt.from_np(value.dtype), kind="ExternalInput").ap())
    args.append(nc.dram_tensor("out_x", (T, D), FP32, kind="ExternalOutput").ap())
    build(nc, *args)
    result = run_bass_kernel_spmd(nc, [feeds], core_ids=[0])
    return result.results[0]["out_x"].reshape(1, T, D)
```

```python
from contextlib import ExitStack

import concourse.bass as bass
from concourse import mybir

FP32 = mybir.dt.float32
FP32R = mybir.dt.float32r
I32 = mybir.dt.int32
ALU = mybir.AluOpType
ACT = mybir.ActivationFunctionType
AX = mybir.AxisListType

D = 1024
T = 256
P = 128
TT = T // P
KC = D // P
DEPTH = 2
ALPHA = (2 * DEPTH) ** 0.25
LN_EPS = 1e-5
HALF = 512
GF = 3 * D
GT = GF // P
HEADS = 8
TILES_PER_HEAD = GT // HEADS
E = 64
GROUPS = 8
PER_GROUP = E // GROUPS
TOPK_GROUPS = 4
ROUTED_SCALE = 2.5
H = 256
HC = H // P
SLOTS = 64
SPAN = SLOTS
QUAD = 4
QUADS = E // QUAD
PASSES = T // SLOTS
RING = 4
HEAD = RING
SLOT = 3 * D * H // P
GU = 2 * D * H // P
NEG = -1e30
SHARE = HALF // QUADS

FILLS = [
    [("a_in", j) for j in range(4)] + [("a_out", 0), ("a_out", 1), ("shared", 0)],
    [("b_in", j) for j in range(8)] + [("b_out", j) for j in range(4)] + [("shared", 1)],
]
FIRST_FILL = [0, len(FILLS[0])]
EXPERT_SLOT = [(len(FILLS[0]) - 1) % RING, (len(FILLS[0]) + len(FILLS[1]) - 1) % RING]
FILL_DMAS = {"a_in": 3, "a_out": 1, "b_in": 1, "b_out": 1, "shared": 2}
ALL_FILLS = FILLS[0] + FILLS[1]


class Named(dict):

    def __getattr__(self, name):
        return self[name]


def fill_ready(n):
    total = sum(FILL_DMAS[ALL_FILLS[m][0]] for m in range(n % RING, n + 1, RING))
    return 16 * (total - 2 if n % RING == 0 else total)


def run_totals(n, head_first, first_slot):
    totals = {"s_ready": n, "gathered": 4 * n, "info_done": n, "xs_ready": 4 * n,
              "info_taken": n, "y_done": 4 * n, "yh_ready": 4 * n, "yl_ready": 4 * n,
              "c_ready": n, "comb_done": 4 * n, "comb_taken": 4 * n + 2}
    totals |= {name: 2 * n for name in ("gu_done", "sig_ready", "gated", "h_ready", "hT_done", "hT_ready")}
    totals |= {f"gu{s}": 32 * n for s in range(RING)}
    totals |= {f"dn{s}": 16 * n for s in range(RING)}
    totals |= {"gu4": 0, "dn4": 0}
    if head_first:
        totals[f"gu{first_slot}"] -= 32
        totals[f"dn{first_slot}"] -= 16
        totals["gu4"], totals["dn4"] = 32, 16
    return totals


def fills_before(n):
    return n // RING


def build(nc, x, xT0, a_w_in, a_conv_w, a_w_out, b_w_in, b_ln, b_wsT, b_w_out, rows, router_w,
          router_bias, w_gate, w_up, w_down, sh_gate, sh_up, sh_down, out):
    ctx = ExitStack()
    with ctx:
        place = [(nc.sbuf_base + 63) // 64 * 64]

        def sb(name, shape, dt=FP32):
            t = nc.alloc_sbuf_tensor_at(name, shape, dt, offset=place[0])
            words = 1
            for n in shape[1:]:
                words *= n
            place[0] += (4 * words + 63) // 64 * 64
            return t

        def sems(prefix, names):
            return Named({n: ctx.enter_context(nc.semaphore(f"{prefix}_{n}")) for n in names.split()})

        ring = sb("ring", [P, RING + 1, SLOT])
        x_tok = sb("x_tok", [P, TT, D])
        xT_at = place[0]
        xT = sb("xT", [P, KC, T])
        xsT = nc.alloc_sbuf_tensor_at("xsT", [P, KC, QUAD * SLOTS], FP32, offset=xT_at)
        acc = sb("acc", [P, TT, D])
        rw = sb("rw", [P, DEPTH, KC, E])
        rb = sb("rb", [P, DEPTH, E])
        row = sb("row", [9, D])
        ident = sb("ident", [P, P])
        ones = sb("ones", [P, P])
        before = sb("before", [P, P])
        causal = sb("causal", [P, P])
        tok = sb("tok", [P, T])
        slot_no = sb("slot_no", [P, QUAD * SLOTS])
        tri_i = sb("tri_i", [P, GROUPS, GROUPS], I32)
        tri = sb("tri", [P, GROUPS, GROUPS])
        own_i = sb("own_i", [P, TT], I32)
        stats = sb("stats", [P, TT, 8, 6])
        mv = sb("mv", [P, TT, 2])
        var_eps = sb("var_eps", [P, TT])
        rstd = sb("rstd", [P, TT])
        minus_half = sb("minus_half", [P, TT])
        shared_base = place[0]
        conv_w = sb("conv_w", [P, KC, 3])
        c_gate = sb("c_gate", [P, 2, T])
        padded = sb("padded", [P, 2, T + 2])
        conv = sb("conv", [P, T])
        aT = sb("aT", [P, KC, T])
        tok_i = sb("tok_i", [P, T], I32)
        slot_i = sb("slot_i", [P, QUAD * SLOTS], I32)
        place[0] = shared_base
        v = sb("v", [P, TT, GF])
        uT = sb("uT", [P, GT, T])
        b_gb = sb("b_gb", [P, 2, GT])
        s_off = sb("s_off", [P, 2, P])
        s_val = sb("s_val", [P, 2, T])
        ws_sum = sb("ws_sum", [P, HEADS, P])
        s_bias = sb("s_bias", [P, HEADS, P])
        wsT = sb("wsT", [P, HEADS, P])
        place[0] = shared_base
        xh = sb("xh", [P, TT, KC, P], FP32R)
        xl = sb("xl", [P, TT, KC, P], FP32R)
        gates = sb("gates", [P, TT, PASSES * E])
        rank = sb("rank", [P, TT, PASSES * E])
        count = sb("count", [P, 1])
        over_f = sb("over_f", [P, 1])
        over = sb("over", [1, 1], I32)
        sel = sb("sel", [P, TT, QUAD * SLOTS], FP32R)
        g_cols = sb("g_cols", [P, TT, QUAD + 1])
        slot_gate = sb("slot_gate", [P, 2])
        slot_tok = sb("slot_tok", [P, 2])
        back = sb("back", [P, 2, T], FP32R)
        sh_dn = sb("sh_dn", [P, HC, D])
        sh_hT = sb("sh_hT", [P, HC, T])
        sig = sb("sig", [P, 2, H])
        gated = sb("gated", [P, 2, H])
        hid = sb("hid", [P, 2, H])
        hidT = sb("hidT", [P, 2, HC * P])
        yh_at = place[0]
        yh = sb("yh", [P, 2, D], FP32R)
        yl = sb("yl", [P, 2, D], FP32R)
        score = sb("score", [P, TT, E])
        biased = sb("biased", [P, TT, E])
        top8 = sb("top8", [P, TT, GROUPS, 8])
        g_score = sb("g_score", [P, TT, GROUPS])
        g_more = sb("g_more", [P, TT, GROUPS, GROUPS])
        g_tied = sb("g_tied", [P, TT, GROUPS, GROUPS])
        g_rank = sb("g_rank", [P, TT, GROUPS])
        masked = sb("masked", [P, TT, E])
        best = sb("best", [P, TT, 8])
        marked = sb("marked", [P, TT, E])
        chosen = sb("chosen", [P, TT, E])
        w_sum = sb("w_sum", [P, TT])
        w_inv = sb("w_inv", [P, TT])
        place[0] = yh_at
        ssig = sb("ssig", [P, TT, H])
        sgated = sb("sgated", [P, TT, H])
        shid = sb("shid", [P, TT, H])
        ps = ctx.enter_context(nc.psum_tensor("ps", [P, 8, HALF], FP32))

        g = sems("g", "xT0 x_in const small row_in ws_in gb_in iotas stored sh_dn first_c first_x load0 load1 load2 load3 vstep")
        load = [g.load0, g.load1, g.load2, g.load3]
        L = [sems(f"l{i}", "proj c_copied a_ready mixed ln_rows ln_var ln_rstd x_ready xT_done xT_ready xh_ready "
                           "xl_ready logits scored chosen ranks over sh_gu sh_sig sh_h sh_hT sh_hT_ready over_ranks "
                           "acc_ready ln2_rows ln2_var ln2_rstd x2_ready x2T_done x2T_ready") for i in range(DEPTH)]
        B = sems("b", "ws_masked sums sums_ready v_proj v_gelu v_var v_rstd v_norm u_proj u_gelu spatial y_ready")
        SECTION = ("s_ready gathered info_done xs_ready info_taken gu_done sig_ready gated h_ready hT_done hT_ready "
                   "y_done yh_ready yl_ready c_ready comb_done comb_taken gu0 gu1 gu2 gu3 gu4 dn0 dn1 dn2 dn3 dn4")
        K = sems("k", SECTION)
        RUNS, at = [], Named({n: 0 for n in SECTION.split()})
        for run in range(2 * DEPTH):
            steps = QUADS if run % 2 == 0 else QUADS * (PASSES - 1)
            k = Named(K, base=Named(at), totals=run_totals(steps, run % 2 == 0, EXPERT_SLOT[run // 2]), steps=steps,
                      layer=run // 2, slot=EXPERT_SLOT[run // 2], head_first=run % 2 == 0,
                      gu_load=[K.gu0, K.gu1, K.gu2, K.gu3, K.gu4], dn_load=[K.dn0, K.dn1, K.dn2, K.dn3, K.dn4])
            RUNS.append(k)
            at = {n: at[n] + k.totals[n] for n in at}
        MAIN, OVER = RUNS[0::2], RUNS[1::2]

        def skip_experts(engine, k, made_here):
            for n in made_here.split():
                engine.sem_inc(K[n], k.totals[n])

        def expert_slot(k, i, j):
            return HEAD if k.head_first and type(i) is int and i == 0 and j == 0 else (k.slot + j) % RING

        def loaded(k, i, s, per, base):
            if k.head_first and s == k.slot:
                return base + i * per
            return base + (i * per + per)

        def slot_gu(s):
            return ring[:, s, 0:GU].rearrange("p (g c h) -> p c g h", g=2, c=KC)

        def slot_dn(s):
            return ring[:, s, GU:SLOT].rearrange("p (k n) -> p k n", k=HC)

        block = ctx.enter_context(nc.Block())

        @block.sync
        def _(sp):
            def load_fill(n):
                kind, j = ALL_FILLS[n]
                s, sem = n % RING, load[n % RING]
                if kind == "a_in":
                    dst = ring[:, s, :].rearrange("p (g c n) -> p g c n", g=3, c=KC)
                    src = a_w_in.rearrange("(p c) (g n) -> p g c n", c=KC, g=3)
                    for gate, first in ((1, g.first_c), (2, g.first_x), (0, sem)):
                        sp.dma_start(dst[:, gate], src[:, gate, :, j * 256:(j + 1) * 256]).then_inc(sem if n else first, 16)
                elif kind == "a_out":
                    tiles = [6, 2][j]
                    dst = ring[:, s, 0:tiles * D].rearrange("p (c n) -> p c n", c=tiles)
                    src = a_w_out.rearrange("(c p) n -> p c n", p=P)
                    sp.dma_start(dst, src[:, 6 * j:6 * j + tiles]).then_inc(sem, 16)
                elif kind == "b_in":
                    first = GF + j * 768 if j < 4 else (j - 4) * 768
                    dst = ring[:, s, :].rearrange("p (c n) -> p c n", c=KC)
                    src = b_w_in.rearrange("(p c) n -> p c n", c=KC)
                    sp.dma_start(dst, src[:, :, first:first + 768]).then_inc(sem, 16)
                elif kind == "b_out":
                    dst = ring[:, s, :].rearrange("p (c n) -> p c n", c=6)
                    src = b_w_out.rearrange("(c p) n -> p c n", p=P)
                    sp.dma_start(dst, src[:, 6 * j:6 * j + 6]).then_inc(sem, 16)
                else:
                    for lo, w in ((0, sh_gate), (GU // 2, sh_up)):
                        sp.dma_start(ring[:, s, lo:lo + GU // 2], w[j].rearrange("(p c) n -> p (c n)", c=KC)).then_inc(sem, 16)

            def wait_used(n):
                kind, j = ALL_FILLS[n]
                if kind == "a_in":
                    sp.wait_ge(L[0].proj, 3 * 2 * (j + 1))
                elif kind == "a_out":
                    sp.wait_ge(L[0].mixed, j + 1)
                elif kind == "b_in":
                    sp.wait_ge(B.v_proj, 4 * (j + 1)) if j < 4 else sp.wait_ge(B.u_proj, 6 * (j - 3))
                elif kind == "b_out":
                    sp.wait_ge(L[1].mixed, j + 1)
                else:
                    sp.wait_ge(L[j].sh_gu, TT)

            def load_expert(layer, s, expert, k, done=None, p=0):
                src = lambda w, c: w[layer, bass.ds(expert, 1)].rearrange("e (p c) n -> (e p) (c n)", c=c)
                if done is not None:
                    sp.wait_ge(k.gu_done, k.base.gu_done + (done * 2 + (p - 1)))
                sp.dma_start(ring[:, s, 0:GU // 2], src(w_gate, KC)).then_inc(k.gu_load[s], 16)
                sp.dma_start(ring[:, s, GU // 2:GU], src(w_up, KC)).then_inc(k.gu_load[s], 16)
                if done is not None:
                    sp.wait_ge(k.y_done, k.base.y_done + (done * 4 + (2 * p - 2)))
                sp.dma_start(ring[:, s, GU:SLOT], src(w_down, HC)).then_inc(k.dn_load[s], 16)

            def load_pair(layer, i, k, done, p):
                src = lambda w, c, j: w[layer, bass.ds(i * QUAD + j, 1)].rearrange("e (p c) n -> (e p) (c n)", c=c)
                sp.wait_ge(k.gu_done, k.base.gu_done + (done * 2 + (p - 1)))
                for j in (2 * p, 2 * p + 1):
                    s = expert_slot(k, i, j)
                    sp.dma_start(ring[:, s, 0:GU // 2], src(w_gate, KC, j)).then_inc(k.gu_load[s], 16)
                    sp.dma_start(ring[:, s, GU // 2:GU], src(w_up, KC, j)).then_inc(k.gu_load[s], 16)
                sp.wait_ge(k.y_done, k.base.y_done + (done * 4 + (2 * p - 2)))
                for j in (2 * p, 2 * p + 1):
                    s = expert_slot(k, i, j)
                    sp.dma_start(ring[:, s, GU:SLOT], src(w_down, HC, j)).then_inc(k.dn_load[s], 16)

            sp.dma_start(xT[:], xT0).then_inc(g.xT0, 16)
            for layer in range(DEPTH):
                for n in range(FIRST_FILL[layer], FIRST_FILL[layer] + len(FILLS[layer])):
                    s = n % RING
                    if layer and n - FIRST_FILL[layer] < RING:
                        pair = (s - EXPERT_SLOT[layer - 1]) % RING // 2
                        sp.wait_ge(MAIN[layer - 1].y_done, MAIN[layer - 1].base.y_done + (4 * (QUADS - 1) + 2 * pair + 2))
                    elif fills_before(n):
                        wait_used(n - RING)
                    load_fill(n)
                k, total = MAIN[layer], FIRST_FILL[layer] + len(FILLS[layer])
                if layer:
                    with sp.If(more > 0):
                        sp.nop()
                    with sp.Else():
                        skip_experts(sp, OVER[0], "gu0 gu1 gu2 gu3 dn0 dn1 dn2 dn3")
                for e in range(QUAD + 1):
                    if e:
                        wait_used(total + e - 1 - RING)
                    load_expert(layer, expert_slot(k, e // QUAD, e % QUAD), e, k)
                load_expert(layer, expert_slot(k, 1, 1), QUAD + 1, k, 1, 0)
                load_pair(layer, 1, k, 1, 1)
                with sp.Fori(2, QUADS) as i:
                    for p in range(2):
                        load_pair(layer, i, k, i, p)
                o = OVER[layer]
                sp.wait_ge(L[layer].over, 1)
                more = sp.value_load(over[0:1, 0:1], min_val=0, max_val=1)
                with sp.If(more > 0):
                    sp.wait_ge(k.y_done, k.base.y_done + (4 * QUADS))
                    for j in range(QUAD):
                        load_expert(layer, expert_slot(o, 0, j), j, o)
                    with sp.Fori(1, QUADS) as i:
                        for p in range(2):
                            load_pair(layer, i, o, i, p)
                    for again in range(2, PASSES):
                        with sp.Fori(0, QUADS) as i:
                            for p in range(2):
                                load_pair(layer, i, o, i + (again - 1) * QUADS, p)
                    sp.wait_ge(o.y_done, o.base.y_done + (4 * QUADS * (PASSES - 1)))
                    sp.nop()
                with sp.Else():
                    sp.nop()
            for t in range(TT):
                sp.wait_ge(L[DEPTH - 1].x2_ready, t + 1)
                sp.dma_start(out[t * P:(t + 1) * P, :], x_tok[:, t, :]).then_inc(g.stored, 16)
            sp.wait_ge(g.stored, 16 * TT)

        @block.gpsimd
        def _(pool):
            nc.gpsimd.memset(ones[:], 1.0).then_inc(g.const, 1)
            nc.gpsimd.memset(minus_half[:], -0.5).then_inc(g.const, 1)
            pool.wait_ge(g.const, 2)
            nc.gpsimd.affine_select(ident[:], ones[:], pattern=[[-1, P]], base=0, channel_multiplier=1,
                                    compare_op=ALU.is_equal, fill=0.0).then_inc(g.const, 1)
            nc.gpsimd.affine_select(before[:], ones[:], pattern=[[1, P]], base=0, channel_multiplier=-1,
                                    compare_op=ALU.is_gt, fill=0.0).then_inc(g.const, 1)
            nc.gpsimd.affine_select(causal[:], ones[:], pattern=[[1, P]], base=0, channel_multiplier=-1,
                                    compare_op=ALU.is_ge, fill=0.0).then_inc(g.const, 1)
            nc.gpsimd.iota(tok_i[:], [[1, T]], base=1, channel_multiplier=0).then_inc(g.iotas, 1)
            nc.gpsimd.iota(slot_i[:], [[0, QUAD], [1, SLOTS]], base=0, channel_multiplier=0).then_inc(g.iotas, 1)
            nc.gpsimd.iota(tri_i[:], [[1, GROUPS], [-1, GROUPS]], base=0, channel_multiplier=0).then_inc(g.iotas, 1)
            nc.gpsimd.iota(own_i[:], [[P, TT]], base=1, channel_multiplier=1).then_inc(g.iotas, 1)
            for layer in range(DEPTH):
                def rsqrt(var_ready, done, n=TT):
                    for t in range(n):
                        pool.wait_ge(var_ready, t + 1)
                        nc.gpsimd.tensor_tensor(rstd[:, t:t + 1], var_eps[:, t:t + 1], minus_half[:, t:t + 1],
                                                ALU.pow).then_inc(done, 1)
                if layer == 1:
                    rsqrt(B.v_var, B.v_rstd)
                rsqrt(L[layer].ln_var, L[layer].ln_rstd)
                if layer == 0:
                    pool.wait_ge(g.ws_in, 16)
                    nc.gpsimd.tensor_tensor(wsT[:], wsT[:], causal[:].unsqueeze(1).to_broadcast([P, HEADS, P]),
                                            ALU.mult).then_inc(B.ws_masked, 1)
                rsqrt(L[layer].ln2_var, L[layer].ln2_rstd)

        @block.tensor
        def _(pe):
            def transposes(ready, done, first_bank):
                for t in range(TT):
                    pe.wait_ge(ready, t + 1)
                    for c in range(KC):
                        bank = first_bank + (t * KC + c) // 4
                        last = nc.tensor.transpose(ps[:, bank, (c % 4) * P:(c % 4 + 1) * P],
                                                   x_tok[:, t, c:D:KC], ident[:])
                        if c % 4 == 3:
                            last.then_inc(done, 1)

            def ln_rows(which, layer, done, bank):
                for j, r in enumerate((4 * layer + 2 * which, 4 * layer + 2 * which + 1)):
                    for h in range(2):
                        last = nc.tensor.matmul(ps[:, bank + 2 * j + h, :], ident[0:9, r:r + 1].to_broadcast([9, P]),
                                                row[:, h * HALF:(h + 1) * HALF], start=True, stop=True)
                last.then_inc(done, 1)

            def gather(q, k, first, count_of):
                for cp in (first, first + 1):
                    free = count_of(4, cp - 1)
                    if free is not None:
                        pe.wait_ge(k.xs_ready, k.base.xs_ready + (free))
                    for c in (2 * cp, 2 * cp + 1):
                        dst = ps[:, 6 + cp % 2, (c % 2) * 256:(c % 2 + 1) * 256]
                        for n, (t, part) in enumerate([(t, part) for t in range(TT) for part in (xh, xl)]):
                            last = nc.tensor.matmul(dst, part[:, t, c, :], sel[:, t, :], start=(n == 0), stop=(n == 3))
                    last.then_inc(k.gathered, 1)

            def slot_info(k):
                for p in range(2):
                    for t in range(TT):
                        last = nc.tensor.matmul(ps[:, 0, 256 + 8 * p:256 + 8 * p + QUAD + 1],
                                                sel[:, t, p * P:(p + 1) * P].bitcast(FP32), g_cols[:, t, :],
                                                start=(t == 0), stop=(t == TT - 1))
                last.then_inc(k.info_done, 1)

            def combine(k, i, groups):
                for n in groups:
                    t, h = n // 2, n % 2
                    pe.wait_ge(k.comb_taken, k.base.comb_taken + (i * 4 + (n - 3)))
                    for p in range(2):
                        for part in (yh, yl):
                            last = nc.tensor.matmul(ps[:, 2 + n % 2, :], back[:, p, t * P:(t + 1) * P],
                                                    part[:, p, h * HALF:(h + 1) * HALF],
                                                    start=(p == 0 and part is yh),
                                                    stop=(p == 1 and part is yl and not k.head_first))
                    if k.head_first:
                        for kk in range(HC):
                            last = nc.tensor.matmul(ps[:, 2 + n % 2, bass.ds((i - 1) * SHARE, SHARE)],
                                                    sh_hT[:, kk, t * P:(t + 1) * P],
                                                    sh_dn[:, kk, bass.ds((i - 1) * SHARE + h * HALF, SHARE)],
                                                    start=False, stop=(kk == HC - 1))
                    last.then_inc(k.comb_done, 1)

            def experts(k, during_first=None, shared=None):
                pe.wait_ge(k.s_ready, k.base.s_ready + (1))
                gather(0, k, 0, lambda per, off: off if off > 0 else None)
                gather(0, k, 2, lambda per, off: off if off > 0 else None)
                slot_info(k)

                def gate_up(i, p):
                    for j in (2 * p, 2 * p + 1):
                        s = expert_slot(k, i, j)
                        pe.wait_ge(k.gu_load[s], loaded(k, i, s, 32, k.base[f"gu{s}"]))
                    for c in range(KC):
                        for half in range(2):
                            s = expert_slot(k, i, 2 * p + half)
                            last = nc.tensor.matmul(ps[64 * half:64 * half + 64, p, :],
                                                    xsT[:, c, (2 * p + half) * SLOTS:(2 * p + half + 1) * SLOTS],
                                                    slot_gu(s)[:, c], start=(c == 0), stop=(c == KC - 1))
                    last.then_inc(k.gu_done, 1)

                def turn(i, p):
                    pe.wait_ge(k.h_ready, k.base.h_ready + (i * 2 + (p + 1)))
                    for kk in range(HC):
                        last = nc.tensor.transpose(ps[:, p, kk * P:(kk + 1) * P], hid[:, p, kk:H:HC], ident[:])
                    last.then_inc(k.hT_done, 1)

                def down(i, p):
                    pe.wait_ge(k.hT_ready, k.base.hT_ready + (i * 2 + (p + 1)))
                    for j in (2 * p, 2 * p + 1):
                        s = expert_slot(k, i, j)
                        pe.wait_ge(k.dn_load[s], loaded(k, i, s, 16, k.base[f"dn{s}"]))
                    for h in range(2):
                        if p == 1:
                            pe.wait_ge(k.yl_ready, k.base.yl_ready + (i * 4 + (h + 1)))
                        for kk in range(HC):
                            for half in range(2):
                                s = expert_slot(k, i, 2 * p + half)
                                last = nc.tensor.matmul(ps[64 * half:64 * half + 64, 4 + h, :],
                                                        hidT[:, p, kk * P + 64 * half:kk * P + 64 * half + 64],
                                                        slot_dn(s)[:, kk, h * HALF:(h + 1) * HALF],
                                                        start=(kk == 0), stop=(kk == HC - 1))
                        last.then_inc(k.y_done, 1)

                def quad(i, first=False, final=False):
                    pe.wait_ge(k.xs_ready, k.base.xs_ready + (i * 4 + 4))
                    pe.wait_ge(k.info_taken, k.base.info_taken + (i + 1))
                    gate_up(i, 0)
                    if not first:
                        pe.wait_ge(k.yl_ready, k.base.yl_ready + (i * 4))
                        pe.wait_ge(k.c_ready, k.base.c_ready + (i))
                        combine(k, i, (0, 1))
                    elif during_first:
                        during_first()
                    turn(i, 0)
                    if not first:
                        combine(k, i, (2, 3))
                    down(i, 0)
                    gate_up(i, 1)
                    if not final:
                        pe.wait_ge(k.s_ready, k.base.s_ready + (i + 2))
                        gather(i, k, 0, lambda per, off: i * 4 + 4 + off)
                    turn(i, 1)
                    if not final:
                        gather(i, k, 2, lambda per, off: i * 4 + 4 + off)
                        slot_info(k)
                    down(i, 1)

                quad(0, first=True)
                if shared:
                    pe.wait_ge(shared.sh_hT_ready, 1)
                    pe.wait_ge(g.sh_dn, 16 * (k.layer + 1))
                with pe.Fori(1, k.steps - 1) as i:
                    quad(i)
                quad(k.steps - 1, final=True)
                pe.wait_ge(k.yl_ready, k.base.yl_ready + k.steps * 4)
                pe.wait_ge(k.c_ready, k.base.c_ready + k.steps)
                combine(k, k.steps, (0, 1, 2, 3))

            pe.wait_ge(g.const, 5)
            pe.wait_ge(g.xT0, 16)
            pe.wait_ge(g.row_in, 16)
            for layer in range(DEPTH):
                W = L[layer]
                if layer == 0:
                    for dt in range(KC):
                        n = dt // 2
                        if dt % 2 == 0 and dt:
                            pe.wait_ge(load[n], fill_ready(n))
                        if dt >= 2:
                            pe.wait_ge(W.a_ready, dt - 1)
                        w = ring[:, n, :].rearrange("p (g c n) -> p g c n", g=3, c=KC)
                        for gate, bank, lo in ((1, 0, 0), (2, 0, 256), (0, 1, 0)):
                            if dt == 0:
                                pe.wait_ge([load[0], g.first_c, g.first_x][gate], 16)
                            for c in range(KC):
                                last = nc.tensor.matmul(ps[:, 2 * (dt % 2) + bank, lo:lo + T],
                                                        w[:, gate, c, (dt % 2) * P:(dt % 2 + 1) * P], xT[:, c, :],
                                                        start=(c == 0), stop=(c == KC - 1))
                            last.then_inc(W.proj, 1)
                    feature_tiles, lhs, ready = KC, aT, W.a_ready
                else:
                    pe.wait_ge(L[0].x2T_ready, 4)
                    for j in range(4):
                        n = FIRST_FILL[1] + j
                        pe.wait_ge(load[n % RING], fill_ready(n))
                        w = ring[:, n % RING, :].rearrange("p (c n) -> p c n", c=KC)
                        for m in range(4):
                            t, nh = m // 2, m % 2
                            u = 4 * j + m
                            if u >= 4:
                                pe.wait_ge(B.v_gelu, u - 3)
                            for c in range(KC):
                                last = nc.tensor.matmul(ps[:, u % 4, 0:384], xT[:, c, t * P:(t + 1) * P],
                                                        w[:, c, nh * 384:(nh + 1) * 384], start=(c == 0), stop=(c == KC - 1))
                            last.then_inc(B.v_proj, 1)
                    for f in range(GT):
                        n = FIRST_FILL[1] + 4 + f // 6
                        if f % 6 == 0:
                            pe.wait_ge(load[n % RING], fill_ready(n))
                        w = ring[:, n % RING, :].rearrange("p (c n) -> p c n", c=KC)
                        pe.wait_ge(B.v_gelu, 16) if f < 4 else pe.wait_ge(B.u_gelu, f - 3)
                        for c in range(KC):
                            last = nc.tensor.matmul(ps[:, f % 4, 0:T], w[:, c, (f % 6) * P:(f % 6 + 1) * P], xT[:, c, :],
                                                    start=(c == 0), stop=(c == KC - 1))
                        last.then_inc(B.u_proj, 1)
                    pe.wait_ge(B.u_gelu, GT)
                    pe.wait_ge(B.v_norm, TT)
                    feature_tiles, lhs, ready = GT, uT, B.y_ready

                def spatial(f):
                    if f >= 4:
                        pe.wait_ge(B.y_ready, f - 3)
                    for t in range(TT):
                        last = nc.tensor.matmul(ps[:, 4 + f % 4, t * P:(t + 1) * P], v[:, t, f * P:(f + 1) * P],
                                                wsT[:, f // TILES_PER_HEAD, :], start=True, stop=True)
                    last.then_inc(B.spatial, 1)

                out_bank = 4 if layer == 0 else 0
                lead = 3
                if layer:
                    for f in range(lead):
                        spatial(f)
                first_out = 4 if layer == 0 else FIRST_FILL[1] + 8
                for f in range(feature_tiles):
                    n = first_out + f // 6
                    if f % 6 == 0:
                        pe.wait_ge(load[n % RING], fill_ready(n))
                    pe.wait_ge(ready, f + 1)
                    w = ring[:, n % RING, :].rearrange("p (c n) -> p c n", c=6)
                    for t in range(TT):
                        for h in range(2):
                            last = nc.tensor.matmul(ps[:, out_bank + 2 * t + h, :], lhs[:, f, t * P:(t + 1) * P],
                                                    w[:, f % 6, h * HALF:(h + 1) * HALF],
                                                    start=(f == 0), stop=(f == feature_tiles - 1))
                    if f % 6 == 5 or f == feature_tiles - 1:
                        last.then_inc(W.mixed, 1)
                    if layer and f + lead < GT:
                        spatial(f + lead)
                ln_rows(0, layer, W.ln_rows, 4 - out_bank)
                transposes(W.x_ready, W.xT_done, out_bank)
                pe.wait_ge(W.x_ready, TT)
                for t in range(TT):
                    pe.wait_ge(W.xT_ready, 2 * t + 2)
                    for c in range(KC):
                        last = nc.tensor.matmul(ps[:, 0, t * E:(t + 1) * E], xT[:, c, t * P:(t + 1) * P], rw[:, layer, c, :],
                                                start=(c == 0), stop=(c == KC - 1))
                last.then_inc(W.logits, 1)
                n = FIRST_FILL[layer] + len(FILLS[layer]) - 1
                s = n % RING
                pe.wait_ge(load[s], fill_ready(n))
                for t in range(TT):
                    for c in range(KC):
                        if t == 1 and c == 2:
                            pe.wait_ge(W.chosen, 1)
                            nc.tensor.matmul(ps[:, 3, 0:E], before[:], chosen[:, 0, :], start=True, stop=True)
                            nc.tensor.matmul(ps[:, 3, E:2 * E], ones[:], chosen[:, 0, :], start=True, stop=False)
                            nc.tensor.matmul(ps[:, 3, E:2 * E], before[:], chosen[:, 1, :], start=False, stop=True)
                            nc.tensor.matmul(ps[:, 3, 2 * E:3 * E], ones[:], chosen[:, 0, :], start=True, stop=False)
                            nc.tensor.matmul(ps[:, 3, 2 * E:3 * E], ones[:], chosen[:, 1, :], start=False,
                                             stop=True).then_inc(W.ranks, 1)
                        last = nc.tensor.matmul(ps[:, 1 + t, :], xT[:, c, t * P:(t + 1) * P], slot_gu(s)[:, c],
                                                start=(c == 0), stop=(c == KC - 1))
                    last.then_inc(W.sh_gu, 1)

                def turn_shared():
                    pe.wait_ge(W.sh_h, TT)
                    pe.wait_ge(W.over, 1)
                    for t in range(TT):
                        for kk in range(HC):
                            last = nc.tensor.transpose(ps[:, 3, kk * T + t * P:kk * T + (t + 1) * P], shid[:, t, kk:H:HC], ident[:])
                    last.then_inc(W.sh_hT, 1)

                pe.wait_ge(W.xl_ready, TT)
                k = MAIN[layer]
                experts(k, turn_shared, W)
                pe.wait_ge(W.over, 1)
                more = pe.value_load(over[0:1, 0:1], min_val=0, max_val=1)
                pe.wait_ge(k.comb_taken, k.base.comb_taken + (4 * QUADS + 2))
                with pe.If(more > 0):
                    experts(OVER[layer])
                    pe.wait_ge(OVER[layer].comb_taken, OVER[layer].base.comb_taken + (4 * QUADS * (PASSES - 1) + 2))
                    pe.nop()
                with pe.Else():
                    if layer == 0:
                        skip_experts(pe, OVER[layer], "gathered info_done gu_done hT_done y_done comb_done")
                    else:
                        pe.nop()
                ln_rows(1, layer, W.ln2_rows, 0)
                if layer + 1 < DEPTH:
                    pe.wait_ge(B.ws_masked, 1)
                    for h in range(2):
                        nc.tensor.matmul(ps[:, 4 + h, :], ones[:], wsT[:, 4 * h:4 * h + 4, :].rearrange("p a b -> p (a b)"),
                                         start=True, stop=True)
                    for h in range(2):
                        last = nc.tensor.matmul(ps[:, 6 + h, :], ident[0:9, 8:9].to_broadcast([9, P]),
                                                row[:, h * HALF:(h + 1) * HALF], start=True, stop=True)
                    last.then_inc(B.sums, 1)
                    pe.wait_ge(B.sums_ready, 2)
                    transposes(W.x2_ready, W.x2T_done, 4)

        @block.scalar
        def _(act):
            def copy_xT(done, ready, bank):
                for n in range(4):
                    act.wait_ge(done, n + 1)
                    t, c = n // 2, 4 * (n % 2)
                    nc.scalar.copy(xT[:, c:c + 4, t * P:(t + 1) * P],
                                   ps[:, bank + n, :].rearrange("p (c t) -> p c t", c=4)).then_inc(ready, 1)

            def experts(k, during_first=None):
                def copy_gathered(n_done, first):
                    for cp in (first, first + 1):
                        act.wait_ge(k.gathered, k.base.gathered + (n_done + (cp + 1)))
                        nc.scalar.copy(xsT[:, 2 * cp:2 * cp + 2, :],
                                       ps[:, 6 + cp % 2, :].rearrange("p (c t) -> p c t", c=2)).then_inc(k.xs_ready, 1)

                def sigmoid(i, p):
                    act.wait_ge(k.gu_done, k.base.gu_done + (i * 2 + (p + 1)))
                    nc.scalar.activation(sig[:, p, :], ps[:, p, 0:H], ACT.Sigmoid).then_inc(k.sig_ready, 1)

                def copy_hT(i, p):
                    act.wait_ge(k.hT_done, k.base.hT_done + (i * 2 + (p + 1)))
                    nc.scalar.copy(hidT[:, p, :], ps[:, p, 0:HC * P]).then_inc(k.hT_ready, 1)

                def high_part(i, p):
                    for h in range(2):
                        act.wait_ge(k.y_done, k.base.y_done + (i * 4 + (2 * p + h + 1)))
                        nc.scalar.copy(yh[:, p, h * HALF:(h + 1) * HALF], ps[:, 4 + h, :]).then_inc(k.yh_ready, 1)

                def quad(i, first=False, final=False):
                    sigmoid(i, 0)
                    if first and during_first:
                        during_first()
                    copy_hT(i, 0)
                    high_part(i, 0)
                    sigmoid(i, 1)
                    if not final:
                        copy_gathered(i * 4 + 4, 0)
                    copy_hT(i, 1)
                    if not final:
                        copy_gathered(i * 4 + 4, 2)
                    high_part(i, 1)

                copy_gathered(0, 0)
                copy_gathered(0, 2)
                quad(0, first=True)
                with act.Fori(1, k.steps - 1) as i:
                    quad(i)
                quad(k.steps - 1, final=True)

            act.dma_start(conv_w[:], a_conv_w).then_inc(g.small, 16)
            act.dma_start(row[:], rows).then_inc(g.row_in, 16)
            act.dma_start(x_tok[:], x.rearrange("(t p) d -> p t d", p=P)).then_inc(g.x_in, 16)
            act.dma_start(rw[:], router_w.rearrange("l (p c) e -> p l c e", c=KC)).then_inc(g.small, 16)
            act.dma_start(rb[:], router_bias.unsqueeze(0).to_broadcast([P, DEPTH, E])).then_inc(g.small, 16)
            for layer in range(DEPTH):
                W = L[layer]
                if layer == 0:
                    for dt in range(KC):
                        act.wait_ge(W.proj, 3 * dt + 2)
                        if dt >= 2:
                            act.wait_ge(W.a_ready, dt - 1)
                        nc.scalar.copy(c_gate[:, dt % 2, :], ps[:, 2 * (dt % 2), 0:T]).then_inc(W.c_copied, 1)
                else:
                    act.dma_start(b_gb[:], b_ln).then_inc(g.gb_in, 16)
                    for u in range(16):
                        j, t, nh = u // 4, (u // 2) % 2, u % 2
                        act.wait_ge(B.v_proj, u + 1)
                        lo = j * 768 + nh * 384
                        nc.scalar.activation(v[:, t, lo:lo + 384], ps[:, u % 4, 0:384],
                                             ACT.Gelu_apprx_tanh).then_inc(B.v_gelu, 1)
                    for f in range(GT):
                        act.wait_ge(B.u_proj, f + 1)
                        nc.scalar.activation(uT[:, f, :], ps[:, f % 4, 0:T], ACT.Gelu_apprx_tanh).then_inc(B.u_gelu, 1)
                act.wait_ge(W.x_ready, 1)
                act.dma_start(sh_dn[:], sh_down[layer].rearrange("(p c) n -> p c n", c=HC)).then_inc(g.sh_dn, 16)
                copy_xT(W.xT_done, W.xT_ready, 0 if layer else 4)
                for t in range(TT):
                    act.wait_ge(W.x_ready, t + 1)
                    nc.scalar.copy(xh[:, t], x_tok[:, t, :].rearrange("p (q c) -> p c q", c=KC)).then_inc(W.xh_ready, 1)
                act.wait_ge(W.logits, 1)
                nc.scalar.activation(score[:].rearrange("p a b -> p (a b)"), ps[:, 0, 0:TT * E],
                                     ACT.Sigmoid).then_inc(W.scored, 1)
                for t in range(TT):
                    act.wait_ge(W.sh_gu, t + 1)
                    nc.scalar.activation(ssig[:, t, :], ps[:, 1 + t, 0:H], ACT.Sigmoid).then_inc(W.sh_sig, 1)
                for t in range(TT):
                    nc.scalar.mul(acc[:, t, :], x_tok[:, t, :], ALPHA).then_inc(W.acc_ready, 1)

                def copy_shared():
                    act.wait_ge(W.sh_hT, 1)
                    nc.scalar.copy(sh_hT[:].rearrange("p a b -> p (a b)"), ps[:, 3, :]).then_inc(W.sh_hT_ready, 1)

                    if layer == 0:
                        act.wait_ge(W.over, 1)
                        act.dma_start(wsT[:], b_wsT).then_inc(g.ws_in, 16)

                experts(MAIN[layer], copy_shared)
                act.wait_ge(W.over, 1)
                more = act.value_load(over[0:1, 0:1], min_val=0, max_val=1)
                with act.If(more > 0):
                    experts(OVER[layer])
                    act.nop()
                with act.Else():
                    if layer == 0:
                        act.wait_ge(W.ln2_rows, 1)
                        skip_experts(act, OVER[layer], "xs_ready sig_ready hT_ready yh_ready")
                    else:
                        act.nop()
                if layer + 1 < DEPTH:
                    act.wait_ge(B.sums, 1)
                    nc.scalar.copy(ws_sum[:].rearrange("p a b -> p (a b)"),
                                   ps[:, 4:6, :].rearrange("p a b -> p (a b)")).then_inc(B.sums_ready, 1)
                    nc.scalar.copy(s_bias[:].rearrange("p a b -> p (a b)"),
                                   ps[:, 6:8, :].rearrange("p a b -> p (a b)")).then_inc(B.sums_ready, 1)
                    copy_xT(W.x2T_done, W.x2T_ready, 4)

        @block.vector
        def _(dve):
            steps_done = [0]

            def step(instruction):
                steps_done[0] += 1
                instruction.then_inc(g.vstep, 1)
                dve.wait_ge(g.vstep, steps_done[0])

            def moments(t, chunks, var_ready):
                step(nc.vector.bn_aggr(mv[:, t, :], stats[:, t, 0:chunks, :].rearrange("p a b -> p (a b)")))
                nc.vector.tensor_scalar(var_eps[:, t:t + 1], mv[:, t, 1:2], LN_EPS, None, ALU.add).then_inc(var_ready, 1)

            def layer_norm(rows_ready, var_ready, rstd_ready, x_ready, bank, residual=None):
                for t in range(TT):
                    if residual:
                        residual(t)
                    for h in range(2):
                        last = nc.vector.bn_stats(stats[:, t, h, :], acc[:, t, h * HALF:(h + 1) * HALF])
                    step(last)
                    moments(t, 2, var_ready)
                    dve.wait_ge(rows_ready, 1)
                    step(nc.vector.scalar_tensor_tensor(acc[:, t, :], acc[:, t, :], mv[:, t, 0:1],
                                                        ps[:, bank:bank + 2, :].rearrange("p a b -> p (a b)"),
                                                        ALU.subtract, ALU.mult))
                    dve.wait_ge(rstd_ready, t + 1)
                    nc.vector.scalar_tensor_tensor(x_tok[:, t, :], acc[:, t, :], rstd[:, t:t + 1],
                                                   ps[:, bank + 2:bank + 4, :].rearrange("p a b -> p (a b)"),
                                                   ALU.mult, ALU.add).then_inc(x_ready, 1)

            def select(k, q):
                for t in range(TT):
                    nc.vector.tensor_tensor(
                        sel[:, t, :].rearrange("p (e s) -> p e s", e=QUAD),
                        slot_no[:].rearrange("p (e s) -> p e s", e=QUAD),
                        rank[:, t, bass.ds(q, QUAD)].unsqueeze(2).to_broadcast([P, QUAD, SLOTS]), ALU.is_equal)
                nc.vector.tensor_copy(g_cols[:, :, 0:QUAD], gates[:, :, bass.ds(q, QUAD)]).then_inc(k.s_ready, 1)

            def take_info(k, n):
                dve.wait_ge(k.info_done, k.base.info_done + (n))
                nc.vector.tensor_copy(slot_gate[0:64, :], ps[0:64, 0, 256:268:10])
                nc.vector.tensor_copy(slot_gate[64:128, :], ps[64:128, 0, 257:268:10])
                nc.vector.tensor_copy(slot_tok[:], ps[:, 0, 260:269:8]).then_inc(k.info_taken, 1)

            def experts(k, first, during_first=None):
                def hidden(i, p):
                    dve.wait_ge(k.sig_ready, k.base.sig_ready + (i * 2 + (p + 1)))
                    nc.vector.scalar_tensor_tensor(gated[:, p, :], sig[:, p, :], slot_gate[:, p:p + 1], ps[:, p, 0:H],
                                                   ALU.mult, ALU.mult).then_inc(k.gated, 1)
                    dve.wait_ge(k.gated, k.base.gated + (i * 2 + (p + 1)))
                    nc.vector.tensor_tensor(hid[:, p, :], gated[:, p, :], ps[:, p, H:2 * H], ALU.mult).then_inc(k.h_ready, 1)

                def low_part(i, p):
                    for h in range(2):
                        dve.wait_ge(k.yh_ready, k.base.yh_ready + (i * 4 + (2 * p + h + 1)))
                        cols = slice(h * HALF, (h + 1) * HALF)
                        nc.vector.tensor_tensor(yl[:, p, cols], ps[:, 4 + h, :], yh[:, p, cols].bitcast(FP32),
                                                ALU.subtract).then_inc(k.yl_ready, 1)

                def add_up(i):
                    for n in range(4):
                        t, h = n // 2, n % 2
                        dve.wait_ge(k.comb_done, k.base.comb_done + (i * 4 + (n - 3)))
                        dve.wait_ge(k.comb_taken, k.base.comb_taken + (i * 4 + (n - 3)))
                        cols = slice(h * HALF, (h + 1) * HALF)
                        nc.vector.tensor_tensor(acc[:, t, cols], acc[:, t, cols], ps[:, 2 + n % 2, :],
                                                ALU.add).then_inc(k.comb_taken, 1)

                def quad(i, start=False, final=False):
                    dve.wait_ge(k.info_taken, k.base.info_taken + (i + 1))
                    hidden(i, 0)
                    if not start:
                        add_up(i)
                    for p in range(2):
                        last = nc.vector.tensor_scalar(back[:, p, :], tok[:], slot_tok[:, p:p + 1], None, ALU.is_equal)
                    last.then_inc(k.c_ready, 1)
                    low_part(i, 0)
                    if not final:
                        dve.wait_ge(k.info_done, k.base.info_done + (i + 1))
                        select(k, i * QUAD + (first + QUAD))
                    hidden(i, 1)
                    if not final:
                        take_info(k, i + 2)
                    low_part(i, 1)

                if during_first:
                    during_first()
                take_info(k, 1)
                quad(0, start=True)
                with dve.Fori(1, k.steps - 1) as i:
                    quad(i)
                quad(k.steps - 1, final=True)
                add_up(k.steps)

            dve.wait_ge(g.iotas, 4)
            nc.vector.tensor_copy(tok[:], tok_i[:])
            nc.vector.tensor_copy(slot_no[:], slot_i[:])
            nc.vector.memset(padded[:, :, 0:2], 0.0)
            step(nc.vector.tensor_scalar(tri[:], tri_i[:], 0, None, ALU.is_gt))
            dve.wait_ge(g.small, 48)
            dve.wait_ge(g.x_in, 16)
            for layer in range(DEPTH):
                W = L[layer]
                if layer == 0:
                    for dt in range(KC):
                        b = dt % 2
                        dve.wait_ge(W.c_copied, dt + 1)
                        step(nc.vector.tensor_tensor(padded[:, b, 2:T + 2], c_gate[:, b, :], ps[:, 2 * b, T:2 * T], ALU.mult))
                        step(nc.vector.tensor_scalar(conv[:], padded[:, b, 2:T + 2], conv_w[:, dt, 2:3], None, ALU.mult))
                        for tap in (1, 0):
                            step(nc.vector.scalar_tensor_tensor(conv[:], padded[:, b, tap:T + tap], conv_w[:, dt, tap:tap + 1],
                                                                conv[:], ALU.mult, ALU.add))
                        dve.wait_ge(W.proj, 3 * dt + 3)
                        nc.vector.tensor_tensor(aT[:, dt, :], conv[:], ps[:, 2 * b + 1, 0:T], ALU.mult).then_inc(W.a_ready, 1)
                    out_bank = 4
                else:
                    for u in range(16):
                        j, t, nh = u // 4, (u // 2) % 2, u % 2
                        dve.wait_ge(B.v_gelu, u + 1)
                        lo = j * 768 + nh * 384
                        last = nc.vector.bn_stats(stats[:, t, 2 * j + nh, :], v[:, t, lo:lo + 384])
                    step(last)
                    for t in range(TT):
                        moments(t, 8, B.v_var)
                    for t in range(TT):
                        dve.wait_ge(B.v_rstd, t + 1)
                        nc.vector.tensor_scalar(v[:, t, :], v[:, t, :], mv[:, t, 0:1], rstd[:, t:t + 1],
                                                ALU.subtract, ALU.mult).then_inc(B.v_norm, 1)
                    dve.wait_ge(B.sums_ready, 2)
                    dve.wait_ge(g.gb_in, 16)
                    for f in range(GT):
                        b, head = f % 2, f // TILES_PER_HEAD
                        step(nc.vector.scalar_tensor_tensor(s_off[:, b, :], ws_sum[:, head, :], b_gb[:, 1, f:f + 1],
                                                            s_bias[:, head, :], ALU.mult, ALU.add))
                        dve.wait_ge(B.spatial, f + 1)
                        step(nc.vector.scalar_tensor_tensor(
                            s_val[:, b, :].rearrange("p (t q) -> p t q", t=TT),
                            ps[:, 4 + f % 4, 0:T].rearrange("p (t q) -> p t q", t=TT), b_gb[:, 0, f:f + 1],
                            s_off[:, b, :].unsqueeze(1).to_broadcast([P, TT, P]), ALU.mult, ALU.add))
                        nc.vector.tensor_tensor(uT[:, f, :], s_val[:, b, :], uT[:, f, :], ALU.mult).then_inc(B.y_ready, 1)
                    out_bank = 0
                dve.wait_ge(W.mixed, 4 if layer else 2)

                def residual(t):
                    step(nc.vector.scalar_tensor_tensor(
                        acc[:, t, :], x_tok[:, t, :], ALPHA,
                        ps[:, out_bank + 2 * t:out_bank + 2 * t + 2, :].rearrange("p a b -> p (a b)"), ALU.mult, ALU.add))

                layer_norm(W.ln_rows, W.ln_var, W.ln_rstd, W.x_ready, 4 - out_bank, residual)
                for t in range(TT):
                    dve.wait_ge(W.xh_ready, t + 1)
                    nc.vector.tensor_tensor(xl[:, t], x_tok[:, t, :].rearrange("p (q c) -> p c q", c=KC),
                                            xh[:, t].bitcast(FP32), ALU.subtract).then_inc(W.xl_ready, 1)
                dve.wait_ge(W.scored, 1)
                step(nc.vector.tensor_tensor(biased[:], score[:], rb[:, layer, :].unsqueeze(1).to_broadcast([P, TT, E]), ALU.add))
                for t in range(TT):
                    for j in range(GROUPS):
                        last = nc.vector.max(top8[:, t, j, :], biased[:, t, j * PER_GROUP:(j + 1) * PER_GROUP])
                step(last)
                step(nc.vector.tensor_tensor(g_score[:], top8[:, :, :, 0], top8[:, :, :, 1], ALU.add))
                other, own = (g_score[:].unsqueeze(2).to_broadcast([P, TT, GROUPS, GROUPS]),
                              g_score[:].unsqueeze(3).to_broadcast([P, TT, GROUPS, GROUPS]))
                step(nc.vector.tensor_tensor(g_more[:], other, own, ALU.is_gt))
                step(nc.vector.tensor_tensor(g_tied[:], other, own, ALU.is_equal))
                step(nc.vector.tensor_tensor(g_tied[:], g_tied[:], tri[:].unsqueeze(1).to_broadcast([P, TT, GROUPS, GROUPS]), ALU.mult))
                step(nc.vector.tensor_tensor(g_more[:], g_more[:], g_tied[:], ALU.add))
                step(nc.vector.reduce_sum(g_rank[:], g_more[:], AX.X))
                step(nc.vector.tensor_scalar(g_rank[:], g_rank[:], TOPK_GROUPS - 0.5, NEG, ALU.is_gt, ALU.mult))
                step(nc.vector.tensor_tensor(
                    masked[:].rearrange("p t (g e) -> p t g e", g=GROUPS), biased[:].rearrange("p t (g e) -> p t g e", g=GROUPS),
                    g_rank[:].unsqueeze(3).to_broadcast([P, TT, GROUPS, PER_GROUP]), ALU.add))
                for t in range(TT):
                    step(nc.vector.max(best[:, t, :], masked[:, t, :]))
                    step(nc.vector.match_replace(marked[:, t, :], best[:, t, :], masked[:, t, :], 4 * NEG))
                nc.vector.tensor_tensor(chosen[:], marked[:], masked[:], ALU.is_lt).then_inc(W.chosen, 1)
                dve.wait_ge(W.chosen, 1)
                step(nc.vector.tensor_tensor(masked[:], score[:], chosen[:], ALU.mult))
                step(nc.vector.reduce_sum(w_sum[:], masked[:], AX.X))
                step(nc.vector.reciprocal(w_inv[:], w_sum[:]))
                for t in range(TT):
                    last = nc.vector.tensor_scalar(gates[:, t, 0:E], masked[:, t, :], w_inv[:, t:t + 1], ROUTED_SCALE,
                                                   ALU.mult, ALU.mult)
                step(last)
                step(nc.vector.tensor_copy(g_cols[:, :, QUAD], own_i[:]))
                dve.wait_ge(W.ranks, 1)
                step(nc.vector.scalar_tensor_tensor(marked[:], ps[:, 3, 0:TT * E].rearrange("p (t e) -> p t e", t=TT), 1.0,
                                                    chosen[:], ALU.add, ALU.mult))
                step(nc.vector.tensor_scalar(rank[:, :, 0:E], marked[:], -1.0, None, ALU.add))
                k = MAIN[layer]
                select(k, 0)
                step(nc.vector.reduce_max(count[:], ps[:, 3, 2 * E:3 * E], AX.X))
                step(nc.vector.tensor_scalar(over_f[:], count[:], SPAN + 0.5, None, ALU.is_gt))
                nc.vector.tensor_copy(over[:], over_f[0:1, :]).then_inc(W.over, 1)
                nc.vector.memset(w_sum[:, 0:1], 0.0).then_inc(k.comb_taken, 2)

                def shared_hidden():
                    for t in range(TT):
                        dve.wait_ge(W.sh_sig, t + 1)
                        step(nc.vector.tensor_tensor(sgated[:, t, :], ssig[:, t, :], ps[:, 1 + t, 0:H], ALU.mult))
                        nc.vector.tensor_tensor(shid[:, t, :], sgated[:, t, :], ps[:, 1 + t, H:2 * H], ALU.mult).then_inc(W.sh_h, 1)

                shared_hidden()
                dve.wait_ge(W.acc_ready, TT)
                experts(k, 0)
                more = dve.value_load(over[0:1, 0:1], min_val=0, max_val=1)
                with dve.If(more > 0):
                    o = OVER[layer]
                    for p in range(1, PASSES):
                        nc.vector.tensor_copy(gates[:, :, p * E:(p + 1) * E], gates[:, :, 0:E])
                        last = nc.vector.tensor_scalar(rank[:, :, p * E:(p + 1) * E], rank[:, :, 0:E], -1.0 * SPAN * p, None, ALU.add)
                    dve.wait_ge(k.comb_taken, k.base.comb_taken + (4 * QUADS + 2))
                    nc.vector.memset(slot_gate[:, 1:2], 0.0).then_inc(o.comb_taken, 2)
                    last.then_inc(W.over_ranks, 1)
                    dve.wait_ge(W.over_ranks, 1)
                    select(o, E)
                    experts(o, E)
                    dve.wait_ge(o.comb_taken, o.base.comb_taken + (4 * QUADS * (PASSES - 1) + 2))
                    dve.nop()
                with dve.Else():
                    if layer == 0:
                        dve.wait_ge(W.ln2_rows, 1)
                        skip_experts(dve, OVER[layer], "s_ready info_taken gated h_ready yl_ready c_ready comb_taken")
                    else:
                        dve.nop()
                dve.wait_ge(k.comb_taken, k.base.comb_taken + (4 * QUADS + 2))
                layer_norm(W.ln2_rows, W.ln2_var, W.ln2_rstd, W.x2_ready, 0)


def kernel(**inputs):
    import concourse.bacc as bacc
    import numpy as np
    from concourse.bass_utils import run_bass_kernel_spmd

    a = {k: np.asarray(v) for k, v in inputs.items()}
    x = np.ascontiguousarray(a["x"][0])
    arrays = {
        "x": x,
        "xT0": np.ascontiguousarray(x.T.reshape(P, KC, T)),
        "a_w_in": a["a_w_in"][0],
        "a_conv_w": np.ascontiguousarray(a["a_conv_w"][0].T.reshape(KC, P, 3).transpose(1, 0, 2)),
        "a_w_out": a["a_w_out"][0],
        "b_w_in": a["b_w_in"][0],
        "b_ln": np.ascontiguousarray(np.stack([a["b_v_ln_g"][0].reshape(GT, P).T, a["b_v_ln_b"][0].reshape(GT, P).T], 1)),
        "b_wsT": np.ascontiguousarray(a["b_w_s"][0].transpose(2, 0, 1)),
        "b_w_out": a["b_w_out"][0],
        "rows": np.stack([a[n][i] for i in range(DEPTH) for n in ("ln1_g", "ln1_b", "ln2_g", "ln2_b")]
                         + [a["b_s_bias"][0].reshape(D)]),
        "router_w": a["router_w"],
        "router_bias": a["router_bias"],
        "w_gate": a["exp_w_gate"],
        "w_up": a["exp_w_up"],
        "w_down": a["exp_w_down"],
        "sh_gate": a["sh_w_gate"],
        "sh_up": a["sh_w_up"],
        "sh_down": a["sh_w_down"],
    }
    nc = bacc.Bacc("TRN2", target_bir_lowering=False, num_devices=1, dynamic_dma_scratch_size=1024)
    feeds, args = {}, []
    for name, value in arrays.items():
        value = np.ascontiguousarray(value)
        feeds[f"in_{name}"] = value
        args.append(nc.dram_tensor(f"in_{name}", value.shape, mybir.dt.from_np(value.dtype), kind="ExternalInput").ap())
    args.append(nc.dram_tensor("out_x", (T, D), FP32, kind="ExternalOutput").ap())
    build(nc, *args)
    result = run_bass_kernel_spmd(nc, [feeds], core_ids=[0])
    return result.results[0]["out_x"].reshape(1, T, D)
```

```python
from contextlib import ExitStack

import concourse.bass as bass
from concourse import mybir

FP32 = mybir.dt.float32
FP32R = mybir.dt.float32r
I32 = mybir.dt.int32
ALU = mybir.AluOpType
ACT = mybir.ActivationFunctionType
AX = mybir.AxisListType

D = 1024
T = 256
P = 128
TT = T // P
KC = D // P
DEPTH = 2
ALPHA = (2 * DEPTH) ** 0.25
LN_EPS = 1e-5
HALF = 512
GF = 3 * D
GT = GF // P
HEADS = 8
TILES_PER_HEAD = GT // HEADS
E = 64
GROUPS = 8
PER_GROUP = E // GROUPS
TOPK_GROUPS = 4
ROUTED_SCALE = 2.5
H = 256
HC = H // P
SLOTS = 64
SPAN = SLOTS
QUAD = 4
QUADS = E // QUAD
PASSES = T // SLOTS
RING = 4
HEAD = RING
SLOT = 3 * D * H // P
GU = 2 * D * H // P
NEG = -1e30
SHARE = HALF // QUADS

FILLS = [
    [("a_in", j) for j in range(4)] + [("a_out", 0), ("a_out", 1), ("shared", 0)],
    [("b_v", j) for j in range(4)] + [(kind, j) for j in range(4) for kind in ("b_u", "b_out")] + [("shared", 1)],
]
PIECES = [
    [(gate, dt) for dt in range(KC) for gate in ("C", "X", "B")] + [("out", dt) for dt in range(KC)],
    [("v", n) for n in range(4 * KC)] + [("u", 0), ("u", 1), ("u", 2)]
    + [piece for f in range(GT) for piece in (("out", f), ("u", f + 3)) if piece[1] < GT],
]
SHARED_BANKS = [5, 2]
BEHIND = 3

FIRST_FILL = [0, len(FILLS[0])]
EXPERT_SLOT = [(len(FILLS[0]) - 1) % RING, (len(FILLS[0]) + len(FILLS[1]) - 1) % RING]
FILL_DMAS = {"a_in": 3, "a_out": 1, "b_v": 1, "b_u": 1, "b_out": 1, "shared": 2}
ALL_FILLS = FILLS[0] + FILLS[1]


class Named(dict):

    def __getattr__(self, name):
        return self[name]


def fill_ready(n):
    total = sum(FILL_DMAS[ALL_FILLS[m][0]] for m in range(n % RING, n + 1, RING))
    return 16 * (total - 2 if n % RING == 0 else total)


def run_totals(n, head_first, first_slot):
    totals = {"s_ready": n, "gathered": 4 * n, "info_done": n, "xs_ready": 4 * n,
              "info_taken": n, "y_done": 4 * n, "yh_ready": 4 * n, "yl_ready": 4 * n,
              "c_ready": n, "comb_done": 4 * n, "comb_taken": 4 * n + 2, "stats_done": 4}
    totals |= {name: 2 * n for name in ("gu_done", "sig_ready", "gated", "h_ready", "hT_done", "hT_ready")}
    totals |= {f"gu{s}": 32 * n for s in range(RING)}
    totals |= {f"dn{s}": 16 * n for s in range(RING)}
    totals |= {"gu4": 0, "dn4": 0}
    if head_first:
        totals[f"gu{first_slot}"] -= 32
        totals[f"dn{first_slot}"] -= 16
        totals["gu4"], totals["dn4"] = 32, 16
    return totals


def fill_of(layer, piece):
    kind, j = piece
    fill = {"C": ("a_in", j // 2), "X": ("a_in", j // 2), "B": ("a_in", j // 2), "v": ("b_v", j // KC),
            "u": ("b_u", j // 6), "out": ("a_out" if layer == 0 else "b_out", j // 6)}[kind]
    return FIRST_FILL[layer] + FILLS[layer].index(fill)


def pieces_done(n):
    layer = n // len(FILLS[0]) and 1
    return 1 + max(i for i, piece in enumerate(PIECES[layer]) if fill_of(layer, piece) == n)


def fills_before(n):
    return n // RING


def build(nc, x, xT0, a_w_in, a_conv_w, a_w_out, b_w_in, b_ln, b_wsT, b_w_out, rows, router_w,
          router_bias, w_gate, w_up, w_down, sh_gate, sh_up, sh_down, out):
    ctx = ExitStack()
    with ctx:
        place = [(nc.sbuf_base + 63) // 64 * 64]

        def sb(name, shape, dt=FP32):
            t = nc.alloc_sbuf_tensor_at(name, shape, dt, offset=place[0])
            words = 1
            for n in shape[1:]:
                words *= n
            place[0] += (4 * words + 63) // 64 * 64
            return t

        def sems(prefix, names):
            return Named({n: ctx.enter_context(nc.semaphore(f"{prefix}_{n}")) for n in names.split()})

        ring_low = [nc.alloc_sbuf_tensor_at(f"ring_low{s}", [P, SLOT], FP32R, offset=place[0] + 4 * SLOT * s) for s in range(RING)]
        ring = sb("ring", [P, RING + 1, SLOT])
        x_tok = sb("x_tok", [P, TT, D])
        xT_at = place[0]
        xT = sb("xT", [P, KC, T])
        xsT = nc.alloc_sbuf_tensor_at("xsT", [P, KC, QUAD * SLOTS], FP32, offset=xT_at)
        acc_at = place[0]
        acc = sb("acc", [P, TT, D])
        xTh = nc.alloc_sbuf_tensor_at("xTh", [P, KC, T], FP32R, offset=xT_at)
        xTl = nc.alloc_sbuf_tensor_at("xTl", [P, KC, T], FP32R, offset=acc_at)
        xT_in = nc.alloc_sbuf_tensor_at("xT_in", [P, KC, T], FP32, offset=acc_at)
        rw = sb("rw", [P, DEPTH, KC, E])
        rb = sb("rb", [P, DEPTH, E])
        row = sb("row", [9, D])
        ident = sb("ident", [P, P])
        ones = sb("ones", [P, P])
        before = sb("before", [P, P])
        causal = sb("causal", [P, P])
        tok = sb("tok", [P, T])
        slot_no = sb("slot_no", [P, QUAD * SLOTS])
        tri_i = sb("tri_i", [P, GROUPS, GROUPS], I32)
        tri = sb("tri", [P, GROUPS, GROUPS])
        own_i = sb("own_i", [P, TT], I32)
        stats = sb("stats", [P, TT, 8, 6])
        mv = sb("mv", [P, TT, 2])
        var_eps = sb("var_eps", [P, TT])
        rstd = sb("rstd", [P, TT])
        minus_half = sb("minus_half", [P, TT])
        shared_base = place[0]
        wh = sb("wh", [P, BEHIND, D], FP32R)
        mixer_base = place[0]
        conv_w = sb("conv_w", [P, KC, 3])
        c_gate = sb("c_gate", [P, 2, T])
        padded = sb("padded", [P, 2, T + 2])
        conv = sb("conv", [P, T])
        aT = sb("aT", [P, 2, T])
        ah = sb("ah", [P, KC, T], FP32R)
        al = sb("al", [P, KC, T], FP32R)
        tok_i = sb("tok_i", [P, T], I32)
        slot_i = sb("slot_i", [P, QUAD * SLOTS], I32)
        place[0] = mixer_base
        v = sb("v", [P, TT, GF])
        uT = sb("uT", [P, 2, T])
        y = sb("y", [P, 2, T])
        yTh = sb("yTh", [P, 2, T], FP32R)
        yTl = sb("yTl", [P, 2, T], FP32R)
        b_gb = sb("b_gb", [P, 2, GT])
        s_off = sb("s_off", [P, 2, P])
        s_val = sb("s_val", [P, 2, T])
        ws_sum = sb("ws_sum", [P, HEADS, P])
        s_bias = sb("s_bias", [P, HEADS, P])
        place[0] = (nc.sbuf_usable_end - 4 * HEADS * P) // 64 * 64
        wsT = sb("wsT", [P, HEADS, P])
        place[0] = shared_base
        xh = sb("xh", [P, TT, KC, P], FP32R)
        xl = sb("xl", [P, TT, KC, P], FP32R)
        gates = sb("gates", [P, TT, PASSES * E])
        rank = sb("rank", [P, TT, PASSES * E])
        count = sb("count", [P, 1])
        over_f = sb("over_f", [P, 1])
        over = sb("over", [1, 1], I32)
        sel = sb("sel", [P, TT, QUAD * SLOTS], FP32R)
        g_cols = sb("g_cols", [P, TT, QUAD + 1])
        slot_gate = sb("slot_gate", [P, 2])
        slot_tok = sb("slot_tok", [P, 2])
        back = sb("back", [P, 2, T], FP32R)
        sh_dn = sb("sh_dn", [P, HC, D])
        sh_hT = sb("sh_hT", [P, HC, T])
        sig = sb("sig", [P, 2, H])
        gated = sb("gated", [P, 2, H])
        hid = sb("hid", [P, 2, H])
        hidT = sb("hidT", [P, 2, HC * P])
        yh_at = place[0]
        yh = sb("yh", [P, 2, D], FP32R)
        yl = sb("yl", [P, 2, D], FP32R)
        score = sb("score", [P, TT, E])
        biased = sb("biased", [P, TT, E])
        top8 = sb("top8", [P, TT, GROUPS, 8])
        g_score = sb("g_score", [P, TT, GROUPS])
        g_more = sb("g_more", [P, TT, GROUPS, GROUPS])
        g_tied = sb("g_tied", [P, TT, GROUPS, GROUPS])
        g_rank = sb("g_rank", [P, TT, GROUPS])
        masked = sb("masked", [P, TT, E])
        best = sb("best", [P, TT, 8])
        marked = sb("marked", [P, TT, E])
        chosen = sb("chosen", [P, TT, E])
        w_sum = sb("w_sum", [P, TT])
        w_inv = sb("w_inv", [P, TT])
        place[0] = yh_at
        ssig = sb("ssig", [P, TT, H])
        sgated = sb("sgated", [P, TT, H])
        shid = sb("shid", [P, TT, H])
        ps = ctx.enter_context(nc.psum_tensor("ps", [P, 8, HALF], FP32))

        g = sems("g", "xT0 x_in const conv_in small row_in ws_in gb_in iotas stored sh_dn first_c first_x load0 load1 load2 load3 vstep")
        load = [g.load0, g.load1, g.load2, g.load3]
        L = [sems(f"l{i}", "x0_high xT_split wh_ready wl_ready used out_done c_copied a_ready ah_ready al_ready ln_rows ln_var ln_rstd x_ready xT_done xT_ready xh_ready "
                           "xl_ready logits scored chosen ranks over sh_gu sh_sig sh_h sh_hT sh_hT_ready over_ranks over_rows first_done "
                           "acc_ready ln2_rows ln2_var ln2_rstd x2_ready x2T_done x2T_ready") for i in range(DEPTH)]
        B = sems("b", "ws_masked sums sums_ready v_gelu v_var v_rstd v_norm u_gelu spatial y_ready yh_ready yl_ready")
        SECTION = ("s_ready gathered info_done xs_ready info_taken gu_done sig_ready gated h_ready hT_done hT_ready "
                   "y_done yh_ready yl_ready c_ready comb_done comb_taken gu0 gu1 gu2 gu3 gu4 dn0 dn1 dn2 dn3 dn4 stats_done")
        K = sems("k", SECTION)
        RUNS, at = [], Named({n: 0 for n in SECTION.split()})
        for run in range(2 * DEPTH):
            steps = QUADS if run % 2 == 0 else QUADS * (PASSES - 1)
            k = Named(K, base=Named(at), totals=run_totals(steps, run % 2 == 0, EXPERT_SLOT[run // 2]), steps=steps,
                      layer=run // 2, slot=EXPERT_SLOT[run // 2], head_first=run % 2 == 0,
                      rows=L[run // 2].over_rows if run % 2 else L[run // 2].ln2_rows, gu_load=[K.gu0, K.gu1, K.gu2, K.gu3, K.gu4], dn_load=[K.dn0, K.dn1, K.dn2, K.dn3, K.dn4])
            RUNS.append(k)
            at = {n: at[n] + k.totals[n] for n in at}
        MAIN, OVER = RUNS[0::2], RUNS[1::2]

        def skip_experts(engine, k, made_here):
            for n in made_here.split():
                engine.sem_inc(K[n], k.totals[n])

        def expert_slot(k, i, j):
            return HEAD if k.head_first and type(i) is int and i == 0 and j == 0 else (k.slot + j) % RING

        def loaded(k, i, s, per, base):
            if k.head_first and s == k.slot:
                return base + i * per
            return base + (i * per + per)

        def product_after(layer, n):
            if layer == 1 and n > 0 and PIECES[1][n - 1][0] == "u":
                return PIECES[1][n - 1][1]
            return None

        def piece_weights(layer, n):
            piece = PIECES[layer][n]
            kind, j = piece
            s = fill_of(layer, piece) % RING
            w, low = piece_of(ring[:, s, :], kind, j), piece_of(ring_low[s][:], kind, j)
            high = wh[:, n % BEHIND, :]
            if kind == "v":
                high = high[:, 0:768]
            elif kind != "out":
                high = high.rearrange("p (c n) -> p c n", c=KC)
            return w, low, high

        def piece_of(slot, kind, j):
            if kind in ("C", "X", "B"):
                cols = slice((j % 2) * P, (j % 2 + 1) * P)
                w = slot.rearrange("p (g c n) -> p g c n", g=3, c=KC)[:, "BCX".index(kind), :, cols]
            elif kind == "u":
                w = slot.rearrange("p (c n) -> p c n", c=KC)[:, :, (j % 6) * P:(j % 6 + 1) * P]
            elif kind == "v":
                w = slot.rearrange("p (c n) -> p c n", c=KC)[:, j % KC, :]
            else:
                w = slot.rearrange("p (c n) -> p c n", c=6)[:, j % 6, :]
            return w

        def slot_gu(s):
            return ring[:, s, 0:GU].rearrange("p (g c h) -> p c g h", g=2, c=KC)

        def slot_dn(s):
            return ring[:, s, GU:SLOT].rearrange("p (k n) -> p k n", k=HC)

        block = ctx.enter_context(nc.Block())

        @block.sync
        def _(sp):
            def load_fill(n):
                kind, j = ALL_FILLS[n]
                s, sem = n % RING, load[n % RING]
                if kind == "a_in":
                    dst = ring[:, s, :].rearrange("p (g c n) -> p g c n", g=3, c=KC)
                    src = a_w_in.rearrange("(p c) (g n) -> p g c n", c=KC, g=3)
                    for gate, first in ((1, g.first_c), (2, g.first_x), (0, sem)):
                        sp.dma_start(dst[:, gate], src[:, gate, :, j * 256:(j + 1) * 256]).then_inc(sem if n else first, 16)
                elif kind == "a_out":
                    tiles = [6, 2][j]
                    dst = ring[:, s, 0:tiles * D].rearrange("p (c n) -> p c n", c=tiles)
                    src = a_w_out.rearrange("(c p) n -> p c n", p=P)
                    sp.dma_start(dst, src[:, 6 * j:6 * j + tiles]).then_inc(sem, 16)
                elif kind in ("b_v", "b_u"):
                    first = j * 768 + (GF if kind == "b_v" else 0)
                    dst = ring[:, s, :].rearrange("p (c n) -> p c n", c=KC)
                    src = b_w_in.rearrange("(p c) n -> p c n", c=KC)
                    sp.dma_start(dst, src[:, :, first:first + 768]).then_inc(sem, 16)
                elif kind == "b_out":
                    dst = ring[:, s, :].rearrange("p (c n) -> p c n", c=6)
                    src = b_w_out.rearrange("(c p) n -> p c n", p=P)
                    sp.dma_start(dst, src[:, 6 * j:6 * j + 6]).then_inc(sem, 16)
                else:
                    for lo, w in ((0, sh_gate), (GU // 2, sh_up)):
                        sp.dma_start(ring[:, s, lo:lo + GU // 2], w[j].rearrange("(p c) n -> p (c n)", c=KC)).then_inc(sem, 16)

            def wait_used(n):
                kind, j = ALL_FILLS[n]
                if kind == "shared":
                    sp.wait_ge(L[j].sh_gu, TT)
                else:
                    layer = 0 if kind in ("a_in", "a_out") else 1
                    if pieces_done(n) < len(PIECES[layer]):
                        sp.wait_ge(L[layer].used, pieces_done(n))
                    else:
                        sp.wait_ge(L[layer].out_done, TT)

            def load_matrix(layer, s, expert, k, w, c, lo, sem):
                src = w[layer, bass.ds(expert, 1)].rearrange("e (p c) n -> (e p) (c n)", c=c)
                sp.dma_start(ring[:, s, lo:lo + GU // 2], src).then_inc(sem[s], 16)

            def load_gate_up(layer, s, expert, k):
                load_matrix(layer, s, expert, k, w_gate, KC, 0, k.gu_load)
                load_matrix(layer, s, expert, k, w_up, KC, GU // 2, k.gu_load)

            def load_down(layer, s, expert, k):
                load_matrix(layer, s, expert, k, w_down, HC, GU, k.dn_load)

            def load_pair(layer, i, k, done, p):
                sp.wait_ge(k.gu_done, k.base.gu_done + (done * 2 + (p - 1)))
                for j in (2 * p, 2 * p + 1):
                    load_gate_up(layer, expert_slot(k, i, j), i * QUAD + j, k)
                sp.wait_ge(k.y_done, k.base.y_done + (done * 4 + (2 * p - 2)))
                for j in (2 * p, 2 * p + 1):
                    load_down(layer, expert_slot(k, i, j), i * QUAD + j, k)

            sp.dma_start(xT_in[:], xT0).then_inc(g.xT0, 16)
            for layer in range(DEPTH):
                for n in range(FIRST_FILL[layer], FIRST_FILL[layer] + len(FILLS[layer])):
                    s = n % RING
                    if layer and n - FIRST_FILL[layer] < RING:
                        pair = (s - EXPERT_SLOT[layer - 1]) % RING // 2
                        sp.wait_ge(MAIN[layer - 1].y_done, MAIN[layer - 1].base.y_done + (4 * (QUADS - 1) + 2 * pair + 2))
                    elif fills_before(n):
                        wait_used(n - RING)
                    load_fill(n)
                k, total = MAIN[layer], FIRST_FILL[layer] + len(FILLS[layer])
                if layer:
                    with sp.If(more > 0):
                        sp.nop()
                    with sp.Else():
                        skip_experts(sp, OVER[0], "gu0 gu1 gu2 gu3 dn0 dn1 dn2 dn3")
                for e in range(QUAD + 1):
                    if e:
                        wait_used(total + e - 1 - RING)
                    s = expert_slot(k, e // QUAD, e % QUAD)
                    load_gate_up(layer, s, e, k)
                    load_down(layer, s, e, k)
                for j in (1, 2, 3):
                    if j < 3:
                        sp.wait_ge(k.gu_done, k.base.gu_done + j)
                    load_gate_up(layer, expert_slot(k, 1, j), QUAD + j, k)
                for j in (1, 2, 3):
                    if j < 3:
                        sp.wait_ge(k.y_done, k.base.y_done + 2 * j)
                    load_down(layer, expert_slot(k, 1, j), QUAD + j, k)
                with sp.Fori(2, QUADS) as i:
                    for p in range(2):
                        load_pair(layer, i, k, i, p)
                o = OVER[layer]
                sp.wait_ge(L[layer].over, 1)
                more = sp.value_load(over[0:1, 0:1], min_val=0, max_val=1)
                with sp.If(more > 0):
                    sp.wait_ge(k.y_done, k.base.y_done + (4 * QUADS))
                    for j in range(QUAD):
                        load_gate_up(layer, expert_slot(o, 0, j), j, o)
                        load_down(layer, expert_slot(o, 0, j), j, o)
                    with sp.Fori(1, QUADS) as i:
                        for p in range(2):
                            load_pair(layer, i, o, i, p)
                    for again in range(2, PASSES):
                        with sp.Fori(0, QUADS) as i:
                            for p in range(2):
                                load_pair(layer, i, o, i + (again - 1) * QUADS, p)
                    sp.wait_ge(o.y_done, o.base.y_done + (4 * QUADS * (PASSES - 1)))
                    sp.nop()
                with sp.Else():
                    sp.nop()
            for t in range(TT):
                sp.wait_ge(L[DEPTH - 1].x2_ready, t + 1)
                sp.dma_start(out[t * P:(t + 1) * P, :], x_tok[:, t, :]).then_inc(g.stored, 16)
            sp.wait_ge(g.stored, 16 * TT)

        @block.gpsimd
        def _(pool):
            nc.gpsimd.memset(ones[:], 1.0).then_inc(g.const, 1)
            nc.gpsimd.memset(minus_half[:], -0.5).then_inc(g.const, 1)
            pool.wait_ge(g.const, 2)
            nc.gpsimd.affine_select(ident[:], ones[:], pattern=[[-1, P]], base=0, channel_multiplier=1,
                                    compare_op=ALU.is_equal, fill=0.0).then_inc(g.const, 1)
            nc.gpsimd.affine_select(before[:], ones[:], pattern=[[1, P]], base=0, channel_multiplier=-1,
                                    compare_op=ALU.is_gt, fill=0.0).then_inc(g.const, 1)
            nc.gpsimd.affine_select(causal[:], ones[:], pattern=[[1, P]], base=0, channel_multiplier=-1,
                                    compare_op=ALU.is_ge, fill=0.0).then_inc(g.const, 1)
            nc.gpsimd.iota(tok_i[:], [[1, T]], base=1, channel_multiplier=0).then_inc(g.iotas, 1)
            nc.gpsimd.iota(slot_i[:], [[0, QUAD], [1, SLOTS]], base=0, channel_multiplier=0).then_inc(g.iotas, 1)
            nc.gpsimd.iota(tri_i[:], [[1, GROUPS], [-1, GROUPS]], base=0, channel_multiplier=0).then_inc(g.iotas, 1)
            nc.gpsimd.iota(own_i[:], [[P, TT]], base=1, channel_multiplier=1).then_inc(g.iotas, 1)
            for layer in range(DEPTH):
                def rsqrt(var_ready, done, n=TT):
                    for t in range(n):
                        pool.wait_ge(var_ready, t + 1)
                        nc.gpsimd.tensor_tensor(rstd[:, t:t + 1], var_eps[:, t:t + 1], minus_half[:, t:t + 1],
                                                ALU.pow).then_inc(done, 1)
                if layer == 1:
                    rsqrt(B.v_var, B.v_rstd)
                rsqrt(L[layer].ln_var, L[layer].ln_rstd)
                if layer == 0:
                    pool.wait_ge(g.ws_in, 16)
                    nc.gpsimd.tensor_tensor(wsT[:], wsT[:], causal[:].unsqueeze(1).to_broadcast([P, HEADS, P]),
                                            ALU.mult).then_inc(B.ws_masked, 1)
                rsqrt(L[layer].ln2_var, L[layer].ln2_rstd)

        @block.tensor
        def _(pe):
            def keep_clock_up(bank, products):
                for _ in range(products):
                    nc.tensor.matmul(ps[:, bank, 0:P], ident[:], ident[:], start=True, stop=True)

            def transposes(t, ready, done):
                pe.wait_ge(ready, t + 1)
                for c in range(KC):
                    bank = 4 + (t * KC + c) // 4
                    last = nc.tensor.transpose(ps[:, bank, (c % 4) * P:(c % 4 + 1) * P],
                                               x_tok[:, t, c:D:KC], ident[:])
                    if c % 4 == 3:
                        last.then_inc(done, 1)

            def ln_row(which, layer, j, done, bank):
                r = 4 * layer + 2 * which + j
                for h in range(2):
                    last = nc.tensor.matmul(ps[:, bank + h, :], ident[0:9, r:r + 1].to_broadcast([9, P]),
                                            row[:, h * HALF:(h + 1) * HALF], start=True, stop=True)
                if done is not None:
                    last.then_inc(done, 1)

            def gather(q, k, first, count_of):
                for cp in (first, first + 1):
                    free = count_of(4, cp - 1)
                    if free is not None:
                        pe.wait_ge(k.xs_ready, k.base.xs_ready + (free))
                    for c in (2 * cp, 2 * cp + 1):
                        dst = ps[:, 6 + cp % 2, (c % 2) * 256:(c % 2 + 1) * 256]
                        for n, (t, part) in enumerate([(t, part) for t in range(TT) for part in (xh, xl)]):
                            last = nc.tensor.matmul(dst, part[:, t, c, :], sel[:, t, :], start=(n == 0), stop=(n == 3))
                    last.then_inc(k.gathered, 1)

            def slot_info(k):
                for p in range(2):
                    for t in range(TT):
                        last = nc.tensor.matmul(ps[:, 0, 256 + 8 * p:256 + 8 * p + QUAD + 1],
                                                sel[:, t, p * P:(p + 1) * P].bitcast(FP32), g_cols[:, t, :],
                                                start=(t == 0), stop=(t == TT - 1))
                last.then_inc(k.info_done, 1)

            def combine(k, i, groups):
                for n in groups:
                    t, h = n // 2, n % 2
                    pe.wait_ge(k.comb_taken, k.base.comb_taken + (i * 4 + (n - 3)))
                    for p in range(2):
                        for part in (yh, yl):
                            last = nc.tensor.matmul(ps[:, 2 + n % 2, :], back[:, p, t * P:(t + 1) * P],
                                                    part[:, p, h * HALF:(h + 1) * HALF],
                                                    start=(p == 0 and part is yh),
                                                    stop=(p == 1 and part is yl and not k.head_first))
                    if k.head_first:
                        for kk in range(HC):
                            last = nc.tensor.matmul(ps[:, 2 + n % 2, bass.ds((i - 1) * SHARE, SHARE)],
                                                    sh_hT[:, kk, t * P:(t + 1) * P],
                                                    sh_dn[:, kk, bass.ds((i - 1) * SHARE + h * HALF, SHARE)],
                                                    start=False, stop=(kk == HC - 1))
                    last.then_inc(k.comb_done, 1)

            def experts(k, during_first=None, shared=None):
                pe.wait_ge(k.s_ready, k.base.s_ready + (1))
                gather(0, k, 0, lambda per, off: off if off > 0 else None)
                gather(0, k, 2, lambda per, off: off if off > 0 else None)
                slot_info(k)

                def gate_up(i, p, first=False):
                    for j in (2 * p, 2 * p + 1):
                        s = expert_slot(k, i, j)
                        pe.wait_ge(k.gu_load[s], loaded(k, i, s, 32, k.base[f"gu{s}"]))
                    for c in range(KC):
                        if first and p == 0 and c % 2 == 0:
                            pe.wait_ge(k.xs_ready, k.base.xs_ready + (c // 2 + 1))
                        for half in range(2):
                            s = expert_slot(k, i, 2 * p + half)
                            last = nc.tensor.matmul(ps[64 * half:64 * half + 64, p, :],
                                                    xsT[:, c, (2 * p + half) * SLOTS:(2 * p + half + 1) * SLOTS],
                                                    slot_gu(s)[:, c], start=(c == 0), stop=(c == KC - 1))
                    last.then_inc(k.gu_done, 1)

                def turn(i, p):
                    pe.wait_ge(k.h_ready, k.base.h_ready + (i * 2 + (p + 1)))
                    for kk in range(HC):
                        last = nc.tensor.transpose(ps[:, p, kk * P:(kk + 1) * P], hid[:, p, kk:H:HC], ident[:])
                    last.then_inc(k.hT_done, 1)

                def down(i, p):
                    pe.wait_ge(k.hT_ready, k.base.hT_ready + (i * 2 + (p + 1)))
                    for j in (2 * p, 2 * p + 1):
                        s = expert_slot(k, i, j)
                        pe.wait_ge(k.dn_load[s], loaded(k, i, s, 16, k.base[f"dn{s}"]))
                    for h in range(2):
                        if p == 1:
                            pe.wait_ge(k.yl_ready, k.base.yl_ready + (i * 4 + (h + 1)))
                        for kk in range(HC):
                            for half in range(2):
                                s = expert_slot(k, i, 2 * p + half)
                                last = nc.tensor.matmul(ps[64 * half:64 * half + 64, 4 + h, :],
                                                        hidT[:, p, kk * P + 64 * half:kk * P + 64 * half + 64],
                                                        slot_dn(s)[:, kk, h * HALF:(h + 1) * HALF],
                                                        start=(kk == 0), stop=(kk == HC - 1))
                        last.then_inc(k.y_done, 1)

                def quad(i, first=False, final=False):
                    if not first:
                        pe.wait_ge(k.xs_ready, k.base.xs_ready + (i * 4 + 4))
                    pe.wait_ge(k.info_taken, k.base.info_taken + (i + 1))
                    gate_up(i, 0, first)
                    if not first:
                        pe.wait_ge(k.yl_ready, k.base.yl_ready + (i * 4))
                        pe.wait_ge(k.c_ready, k.base.c_ready + (i))
                        combine(k, i, (0, 1))
                    else:
                        gate_up(i, 1)
                        if during_first:
                            during_first()
                    turn(i, 0)
                    if not first:
                        combine(k, i, (2, 3))
                    down(i, 0)
                    if not first:
                        gate_up(i, 1)
                    if not final:
                        pe.wait_ge(k.s_ready, k.base.s_ready + (i + 2))
                        gather(i, k, 0, lambda per, off: i * 4 + 4 + off)
                    else:
                        ln_row(1, k.layer, 0, k.rows, 6)
                    turn(i, 1)
                    if not final:
                        gather(i, k, 2, lambda per, off: i * 4 + 4 + off)
                        slot_info(k)
                    down(i, 1)
                    if final:
                        ln_row(1, k.layer, 1, k.rows, 0)

                quad(0, first=True)
                if shared:
                    pe.wait_ge(shared.sh_hT_ready, 1)
                    pe.wait_ge(g.sh_dn, 16 * (k.layer + 1))
                with pe.Fori(1, k.steps - 1) as i:
                    quad(i)
                quad(k.steps - 1, final=True)
                pe.wait_ge(k.yl_ready, k.base.yl_ready + k.steps * 4)
                pe.wait_ge(k.c_ready, k.base.c_ready + k.steps)
                combine(k, k.steps, (0, 1, 2, 3))

            pe.wait_ge(g.const, 5)
            keep_clock_up(7, 18)
            pe.wait_ge(g.row_in, 16)
            for layer in range(DEPTH):
                W = L[layer]
                pe.wait_ge(W.xT_split, 1 if layer == 0 else 4)

                def columns(dst, wh_n, wl_n):
                    for c in range(KC):
                        for a, b in ((wh_n, xTh), (wh_n, xTl), (wl_n, xTh)):
                            last = nc.tensor.matmul(dst, a[:, c, :], b[:, c, :], start=(c == 0 and b is xTh and a is wh_n),
                                                    stop=(c == KC - 1 and a is wl_n))
                    return last

                def output(n, t):
                    _, wl_n, wh_n = piece_weights(layer, n)
                    j = PIECES[layer][n][1]
                    high, low = (ah[:, j, :], al[:, j, :]) if layer == 0 else (yTh[:, j % 2, :], yTl[:, j % 2, :])
                    for h in range(2):
                        cols = slice(h * HALF, (h + 1) * HALF)
                        for a, b in ((high, wh_n), (low, wh_n), (high, wl_n)):
                            last = nc.tensor.matmul(ps[:, 4 + 2 * t + h, :], a[:, t * P:(t + 1) * P], b[:, cols],
                                                    start=(j == 0 and a is high and b is wh_n),
                                                    stop=(n == len(PIECES[layer]) - 1 and b is wl_n))
                    return last

                for n, (kind, j) in enumerate(PIECES[layer]):
                    _, wl_n, wh_n = piece_weights(layer, n)
                    pe.wait_ge(W.wl_ready, n + 1)
                    if kind in ("C", "X", "B"):
                        if kind == "C" and j >= 2:
                            pe.wait_ge(W.a_ready, j - 1)
                        bank, lo = {"C": (0, 0), "X": (0, T), "B": (1, 0)}[kind]
                        last = columns(ps[:, 2 * (j % 2) + bank, lo:lo + T], wh_n, wl_n)
                    elif kind == "v":
                        c, first = j % KC, 4 * (j // KC % 2)
                        if c == 0 and j // KC >= 2:
                            pe.wait_ge(B.v_gelu, 4 * (j // KC - 1))
                        for m in range(4):
                            t, nh = m // 2, m % 2
                            cols = slice(nh * 384, (nh + 1) * 384)
                            for a, b in ((xTh, wh_n), (xTl, wh_n), (xTh, wl_n)):
                                last = nc.tensor.matmul(ps[:, first + m, 0:384], a[:, c, t * P:(t + 1) * P], b[:, cols],
                                                        start=(c == 0 and a is xTh and b is wh_n),
                                                        stop=(c == KC - 1 and b is wl_n))
                    elif kind == "u":
                        if j >= 2:
                            pe.wait_ge(B.u_gelu, j - 1)
                        last = columns(ps[:, j % 2, 0:T], wh_n, wl_n)
                    else:
                        pe.wait_ge(W.al_ready if layer == 0 else B.yl_ready, j + 1)
                        if n == len(PIECES[layer]) - 2:
                            continue
                        if n < len(PIECES[layer]) - 2:
                            for t in range(TT):
                                last = output(n, t)
                        else:
                            for t in range(TT):
                                output(n - 1, t)
                                last = output(n, t)
                                last.then_inc(W.out_done, 1)
                                ln_row(0, layer, t, W.ln_rows, 2 * t)
                            break
                    last.then_inc(W.used, 1)
                    if kind == "u" and j >= 1:
                        for f in ((0, 1) if j == 1 else (j,)):
                            if f % 6 == 0:
                                pe.wait_ge(B.v_norm, TT * (f // 6 + 1))
                            if f >= 2:
                                pe.wait_ge(B.y_ready, f - 1)
                            for t in range(TT):
                                last = nc.tensor.matmul(ps[:, 2 + f % 2, t * P:(t + 1) * P], v[:, t, f * P:(f + 1) * P],
                                                        wsT[:, f // TILES_PER_HEAD, :], start=True, stop=True)
                            last.then_inc(B.spatial, 1)
                n = FIRST_FILL[layer] + len(FILLS[layer]) - 1
                s = n % RING

                def router(t):
                    pe.wait_ge(W.xT_ready, 2 * t + 2)
                    for c in range(KC):
                        last = nc.tensor.matmul(ps[:, 4, t * E:(t + 1) * E], xT[:, c, t * P:(t + 1) * P], rw[:, layer, c, :],
                                                start=(c == 0), stop=(c == KC - 1))
                    return last

                def shared_gate_up(t, chunks):
                    for c in chunks:
                        last = nc.tensor.matmul(ps[:, SHARED_BANKS[t], :], xT[:, c, t * P:(t + 1) * P], slot_gu(s)[:, c],
                                                start=(c == 0), stop=(c == KC - 1))
                    if c == KC - 1:
                        last.then_inc(W.sh_gu, 1)

                pe.wait_ge(W.ln_var, 1)
                keep_clock_up(4, 12)
                transposes(0, W.x_ready, W.xT_done)
                transposes(1, W.x_ready, W.xT_done)
                pe.wait_ge(g.small, 32)
                router(0)
                router(1).then_inc(W.logits, 1)
                pe.wait_ge(load[s], fill_ready(n))
                shared_gate_up(0, range(0, KC))
                shared_gate_up(1, range(0, 3))
                pe.wait_ge(W.chosen, 1)
                nc.tensor.matmul(ps[:, 3, 0:E], before[:], chosen[:, 0, :], start=True, stop=True)
                nc.tensor.matmul(ps[:, 3, E:2 * E], ones[:], chosen[:, 0, :], start=True, stop=False)
                nc.tensor.matmul(ps[:, 3, E:2 * E], before[:], chosen[:, 1, :], start=False, stop=True)
                nc.tensor.matmul(ps[:, 3, 2 * E:3 * E], ones[:], chosen[:, 0, :], start=True, stop=False)
                nc.tensor.matmul(ps[:, 3, 2 * E:3 * E], ones[:], chosen[:, 1, :], start=False,
                                 stop=True).then_inc(W.ranks, 1)
                shared_gate_up(1, range(3, KC))

                def turn_shared():
                    pe.wait_ge(W.sh_h, TT)
                    pe.wait_ge(W.over, 1)
                    for t in range(TT):
                        for kk in range(HC):
                            last = nc.tensor.transpose(ps[:, 3, kk * T + t * P:kk * T + (t + 1) * P], shid[:, t, kk:H:HC], ident[:])
                    last.then_inc(W.sh_hT, 1)

                pe.wait_ge(W.xl_ready, TT)
                k = MAIN[layer]
                experts(k, turn_shared, W)
                pe.wait_ge(W.over, 1)
                more = pe.value_load(over[0:1, 0:1], min_val=0, max_val=1)
                pe.wait_ge(k.comb_taken, k.base.comb_taken + (4 * QUADS + 2))
                pe.sem_inc(W.first_done, 1)
                with pe.If(more > 0):
                    experts(OVER[layer])
                    pe.wait_ge(OVER[layer].comb_taken, OVER[layer].base.comb_taken + (4 * QUADS * (PASSES - 1) + 2))
                    pe.nop()
                with pe.Else():
                    if layer == 0:
                        skip_experts(pe, OVER[layer], "gathered info_done gu_done hT_done y_done comb_done")
                    else:
                        pe.nop()
                if layer + 1 < DEPTH:
                    pe.wait_ge(B.ws_masked, 1)
                    for h in range(2):
                        nc.tensor.matmul(ps[:, 2 + h, :], ones[:], wsT[:, 4 * h:4 * h + 4, :].rearrange("p a b -> p (a b)"),
                                         start=True, stop=True)
                    for h in range(2):
                        last = nc.tensor.matmul(ps[:, 4 + h, :], ident[0:9, 8:9].to_broadcast([9, P]),
                                                row[:, h * HALF:(h + 1) * HALF], start=True, stop=True)
                    last.then_inc(B.sums, 1)
                    pe.wait_ge(B.sums_ready, 2)
                    for t in range(TT):
                        transposes(t, W.x2_ready, W.x2T_done)

        @block.scalar
        def _(act):
            def split_high(layer, n):
                fill = fill_of(layer, PIECES[layer][n])
                if fill == 0:
                    if n < 3:
                        act.wait_ge([g.first_c, g.first_x, load[0]][n], 16)
                elif n == 0 or fill_of(layer, PIECES[layer][n - 1]) != fill:
                    act.wait_ge(load[fill % RING], fill_ready(fill))
                w, _, wh_n = piece_weights(layer, n)
                nc.scalar.copy(wh_n, w).then_inc(L[layer].wh_ready, 1)

            def copy_xT(done, ready, xT, banks=(0, 1, 2, 3)):
                for n in banks:
                    act.wait_ge(done, n + 1)
                    t, c = n // 2, 4 * (n % 2)
                    nc.scalar.copy(xT[:, c:c + 4, t * P:(t + 1) * P],
                                   ps[:, 4 + n, :].rearrange("p (c t) -> p c t", c=4)).then_inc(ready, 1)

            def experts(k, during_first=None):
                def copy_gathered(n_done, first):
                    for cp in (first, first + 1):
                        act.wait_ge(k.gathered, k.base.gathered + (n_done + (cp + 1)))
                        nc.scalar.copy(xsT[:, 2 * cp:2 * cp + 2, :],
                                       ps[:, 6 + cp % 2, :].rearrange("p (c t) -> p c t", c=2)).then_inc(k.xs_ready, 1)

                def sigmoid(i, p):
                    act.wait_ge(k.gu_done, k.base.gu_done + (i * 2 + (p + 1)))
                    nc.scalar.activation(sig[:, p, :], ps[:, p, 0:H], ACT.Sigmoid).then_inc(k.sig_ready, 1)

                def copy_hT(i, p):
                    act.wait_ge(k.hT_done, k.base.hT_done + (i * 2 + (p + 1)))
                    nc.scalar.copy(hidT[:, p, :], ps[:, p, 0:HC * P]).then_inc(k.hT_ready, 1)

                def high_part(i, p):
                    for h in range(2):
                        act.wait_ge(k.y_done, k.base.y_done + (i * 4 + (2 * p + h + 1)))
                        nc.scalar.copy(yh[:, p, h * HALF:(h + 1) * HALF], ps[:, 4 + h, :]).then_inc(k.yh_ready, 1)

                def quad(i, first=False, final=False):
                    sigmoid(i, 0)
                    if first:
                        sigmoid(i, 1)
                        if during_first:
                            during_first()
                    copy_hT(i, 0)
                    high_part(i, 0)
                    if not first:
                        sigmoid(i, 1)
                    if not final:
                        copy_gathered(i * 4 + 4, 0)
                    copy_hT(i, 1)
                    if not final:
                        copy_gathered(i * 4 + 4, 2)
                    high_part(i, 1)

                copy_gathered(0, 0)
                copy_gathered(0, 2)
                quad(0, first=True)
                if k.head_first:
                    for t in range(TT):
                        nc.scalar.mul(acc[:, t, :], x_tok[:, t, :], ALPHA).then_inc(L[k.layer].acc_ready, 1)
                with act.Fori(1, k.steps - 1) as i:
                    quad(i)
                quad(k.steps - 1, final=True)

            act.dma_start(conv_w[:], a_conv_w).then_inc(g.conv_in, 16)
            act.dma_start(row[:], rows).then_inc(g.row_in, 16)
            for layer in range(DEPTH):
                W = L[layer]
                if layer == 0:
                    act.wait_ge(g.xT0, 16)
                    nc.scalar.copy(xTh[:], xT_in[:]).then_inc(L[0].x0_high, 1)
                else:
                    act.dma_start(b_gb[:], b_ln).then_inc(g.gb_in, 16)

                def duty(n):
                    kind, j = PIECES[layer][n]
                    f = product_after(layer, n)
                    if f is not None:
                        act.wait_ge(B.y_ready, f + 1)
                        nc.scalar.copy(yTh[:, f % 2, :], y[:, f % 2, :]).then_inc(B.yh_ready, 1)
                    if kind == "X":
                        nc.scalar.copy(c_gate[:, j % 2, :], ps[:, 2 * (j % 2), 0:T]).then_inc(W.c_copied, 1)
                    elif kind == "C" and j or kind == "out" and j == 0 and layer == 0:
                        dt = j - 1 if kind == "C" else KC - 1
                        act.wait_ge(W.a_ready, dt + 1)
                        nc.scalar.copy(ah[:, dt, :], aT[:, dt % 2, :]).then_inc(W.ah_ready, 1)
                    elif kind == "v" and j % KC == KC - 1:
                        for m in range(4):
                            t, nh = m // 2, m % 2
                            lo = (j // KC) * 768 + nh * 384
                            nc.scalar.activation(v[:, t, lo:lo + 384], ps[:, 4 * (j // KC % 2) + m, 0:384],
                                                 ACT.Gelu_apprx_tanh).then_inc(B.v_gelu, 1)
                    if kind == "u":
                        if j >= 2:
                            act.wait_ge(B.y_ready, j - 1)
                        nc.scalar.activation(uT[:, j % 2, :], ps[:, j % 2, 0:T], ACT.Gelu_apprx_tanh).then_inc(B.u_gelu, 1)

                for n in range(len(PIECES[layer]) + 1):
                    if layer == 0 and n == 6:
                        act.dma_start(x_tok[:], x.rearrange("(t p) d -> p t d", p=P)).then_inc(g.x_in, 16)
                        act.dma_start(rw[:], router_w.rearrange("l (p c) e -> p l c e", c=KC)).then_inc(g.small, 16)
                        act.dma_start(rb[:], router_bias.unsqueeze(0).to_broadcast([P, DEPTH, E])).then_inc(g.small, 16)
                    if n >= BEHIND:
                        act.wait_ge(W.used, n - BEHIND + 1)
                    if n < len(PIECES[layer]) and not (layer and n == 0):
                        split_high(layer, n)
                    if n >= BEHIND:
                        duty(n - BEHIND)
                act.wait_ge(W.x_ready, 1)
                act.wait_ge(W.out_done, TT)
                act.dma_start(sh_dn[:], sh_down[layer].rearrange("(p c) n -> p c n", c=HC)).then_inc(g.sh_dn, 16)
                def copy_high(t):
                    act.wait_ge(W.x_ready, t + 1)
                    nc.scalar.copy(xh[:, t], x_tok[:, t, :].rearrange("p (q c) -> p c q", c=KC)).then_inc(W.xh_ready, 1)

                copy_xT(W.xT_done, W.xT_ready, xT, (0, 1))
                copy_high(0)
                copy_xT(W.xT_done, W.xT_ready, xT, (2, 3))
                act.wait_ge(W.logits, 1)
                nc.scalar.activation(score[:].rearrange("p a b -> p (a b)"), ps[:, 4, 0:TT * E],
                                     ACT.Sigmoid).then_inc(W.scored, 1)
                copy_high(1)
                for t in range(TT):
                    act.wait_ge(W.sh_gu, t + 1)
                    nc.scalar.activation(ssig[:, t, :], ps[:, SHARED_BANKS[t], 0:H], ACT.Sigmoid).then_inc(W.sh_sig, 1)

                def copy_shared():
                    act.wait_ge(W.sh_hT, 1)
                    nc.scalar.copy(sh_hT[:].rearrange("p a b -> p (a b)"), ps[:, 3, :]).then_inc(W.sh_hT_ready, 1)

                    if layer == 0:
                        act.wait_ge(W.over, 1)
                        act.dma_start(wsT[:], b_wsT).then_inc(g.ws_in, 16)

                experts(MAIN[layer], copy_shared)
                act.wait_ge(W.over, 1)
                more = act.value_load(over[0:1, 0:1], min_val=0, max_val=1)
                with act.If(more > 0):
                    experts(OVER[layer])
                    act.nop()
                with act.Else():
                    if layer == 0:
                        act.wait_ge(W.first_done, 1)
                        skip_experts(act, OVER[layer], "xs_ready sig_ready hT_ready yh_ready")
                    else:
                        act.nop()
                if layer + 1 < DEPTH:
                    act.wait_ge(B.sums, 1)
                    nc.scalar.copy(ws_sum[:].rearrange("p a b -> p (a b)"),
                                   ps[:, 2:4, :].rearrange("p a b -> p (a b)")).then_inc(B.sums_ready, 1)
                    nc.scalar.copy(s_bias[:].rearrange("p a b -> p (a b)"),
                                   ps[:, 4:6, :].rearrange("p a b -> p (a b)")).then_inc(B.sums_ready, 1)
                    split_high(1, 0)
                    copy_xT(W.x2T_done, W.x2T_ready, xTh)

        @block.vector
        def _(dve):
            steps_done = [0]

            def step(instruction):
                steps_done[0] += 1
                instruction.then_inc(g.vstep, 1)
                dve.wait_ge(g.vstep, steps_done[0])

            def split_low(layer, n):
                dve.wait_ge(L[layer].wh_ready, n + 1)
                w, wl_n, wh_n = piece_weights(layer, n)
                nc.vector.tensor_tensor(wl_n, w, wh_n.bitcast(FP32), ALU.subtract).then_inc(L[layer].wl_ready, 1)

            def moments(t, chunks, var_ready):
                step(nc.vector.bn_aggr(mv[:, t, :], stats[:, t, 0:chunks, :].rearrange("p a b -> p (a b)")))
                nc.vector.tensor_scalar(var_eps[:, t:t + 1], mv[:, t, 1:2], LN_EPS, None, ALU.add).then_inc(var_ready, 1)

            def layer_norm(rows_ready, var_ready, rstd_ready, x_ready, gain, bias, residual=None):
                def rows_of(bank):
                    return ps[:, bank:bank + 2, :].rearrange("p a b -> p (a b)")

                def statistics(t):
                    if residual:
                        residual(t)
                        for h in range(2):
                            last = nc.vector.bn_stats(stats[:, t, h, :], acc[:, t, h * HALF:(h + 1) * HALF])
                        step(last)
                    moments(t, 2, var_ready)

                def centre(t):
                    dve.wait_ge(rows_ready, 1)
                    return nc.vector.scalar_tensor_tensor(acc[:, t, :], acc[:, t, :], mv[:, t, 0:1], rows_of(gain),
                                                          ALU.subtract, ALU.mult)

                def scale(t):
                    dve.wait_ge(rstd_ready, t + 1)
                    dve.wait_ge(rows_ready, 2)
                    nc.vector.scalar_tensor_tensor(x_tok[:, t, :], acc[:, t, :], rstd[:, t:t + 1], rows_of(bias),
                                                   ALU.mult, ALU.add).then_inc(x_ready, 1)

                statistics(0)
                step(centre(0))
                if residual:
                    statistics(1)
                    scale(0)
                else:
                    scale(0)
                    statistics(1)
                step(centre(1))
                scale(1)

            def select(k, q):
                for t in range(TT):
                    nc.vector.tensor_tensor(
                        sel[:, t, :].rearrange("p (e s) -> p e s", e=QUAD),
                        slot_no[:].rearrange("p (e s) -> p e s", e=QUAD),
                        rank[:, t, bass.ds(q, QUAD)].unsqueeze(2).to_broadcast([P, QUAD, SLOTS]), ALU.is_equal)
                nc.vector.tensor_copy(g_cols[:, :, 0:QUAD], gates[:, :, bass.ds(q, QUAD)]).then_inc(k.s_ready, 1)

            def take_info(k, n):
                dve.wait_ge(k.info_done, k.base.info_done + (n))
                nc.vector.tensor_copy(slot_gate[0:64, :], ps[0:64, 0, 256:268:10])
                nc.vector.tensor_copy(slot_gate[64:128, :], ps[64:128, 0, 257:268:10])
                nc.vector.tensor_copy(slot_tok[:], ps[:, 0, 260:269:8]).then_inc(k.info_taken, 1)

            def experts(k, first, during_first=None):
                def hidden(i, p):
                    dve.wait_ge(k.sig_ready, k.base.sig_ready + (i * 2 + (p + 1)))
                    nc.vector.scalar_tensor_tensor(gated[:, p, :], sig[:, p, :], slot_gate[:, p:p + 1], ps[:, p, 0:H],
                                                   ALU.mult, ALU.mult).then_inc(k.gated, 1)
                    dve.wait_ge(k.gated, k.base.gated + (i * 2 + (p + 1)))
                    nc.vector.tensor_tensor(hid[:, p, :], gated[:, p, :], ps[:, p, H:2 * H], ALU.mult).then_inc(k.h_ready, 1)

                def low_part(i, p):
                    for h in range(2):
                        dve.wait_ge(k.yh_ready, k.base.yh_ready + (i * 4 + (2 * p + h + 1)))
                        cols = slice(h * HALF, (h + 1) * HALF)
                        nc.vector.tensor_tensor(yl[:, p, cols], ps[:, 4 + h, :], yh[:, p, cols].bitcast(FP32),
                                                ALU.subtract).then_inc(k.yl_ready, 1)

                def add_up(i, final=False):
                    for n in range(4):
                        t, h = n // 2, n % 2
                        dve.wait_ge(k.comb_done, k.base.comb_done + (i * 4 + (n - 3)))
                        dve.wait_ge(k.comb_taken, k.base.comb_taken + (i * 4 + (n - 3)))
                        cols = slice(h * HALF, (h + 1) * HALF)
                        nc.vector.tensor_tensor(acc[:, t, cols], acc[:, t, cols], ps[:, 2 + n % 2, :],
                                                ALU.add).then_inc(k.comb_taken, 1)
                        if final:
                            dve.wait_ge(k.comb_taken, k.base.comb_taken + (i * 4 + (n - 1)))
                            nc.vector.bn_stats(stats[:, t, h, :], acc[:, t, cols]).then_inc(k.stats_done, 1)

                def quad(i, start=False, final=False):
                    dve.wait_ge(k.info_taken, k.base.info_taken + (i + 1))
                    hidden(i, 0)
                    if start:
                        hidden(i, 1)
                    else:
                        add_up(i)
                    for p in range(2):
                        last = nc.vector.tensor_scalar(back[:, p, :], tok[:], slot_tok[:, p:p + 1], None, ALU.is_equal)
                    last.then_inc(k.c_ready, 1)
                    low_part(i, 0)
                    if not final:
                        dve.wait_ge(k.info_done, k.base.info_done + (i + 1))
                        select(k, i * QUAD + (first + QUAD))
                    if not start:
                        hidden(i, 1)
                    if not final:
                        take_info(k, i + 2)
                    low_part(i, 1)

                if during_first:
                    during_first()
                take_info(k, 1)
                quad(0, start=True)
                if k.head_first:
                    dve.wait_ge(L[k.layer].acc_ready, TT)
                with dve.Fori(1, k.steps - 1) as i:
                    quad(i)
                quad(k.steps - 1, final=True)
                add_up(k.steps, final=True)

            dve.wait_ge(g.iotas, 4)
            nc.vector.tensor_copy(tok[:], tok_i[:])
            nc.vector.tensor_copy(slot_no[:], slot_i[:])
            nc.vector.memset(padded[:, :, 0:2], 0.0)
            step(nc.vector.tensor_scalar(tri[:], tri_i[:], 0, None, ALU.is_gt))
            for layer in range(DEPTH):
                W = L[layer]
                if layer == 0:
                    dve.wait_ge(g.conv_in, 16)
                    dve.wait_ge(W.x0_high, 1)
                    nc.vector.tensor_tensor(xTl[:], xT_in[:], xTh[:].bitcast(FP32), ALU.subtract).then_inc(W.xT_split, 1)
                else:
                    dve.wait_ge(L[0].x2_ready, TT)
                    split_low(1, 0)
                    for n in range(4):
                        dve.wait_ge(L[0].x2T_ready, n + 1)
                        t, c = n // 2, 4 * (n % 2)
                        nc.vector.tensor_tensor(xTl[:, c:c + 4, t * P:(t + 1) * P], ps[:, 4 + n, :].rearrange("p (c t) -> p c t", c=4),
                                                xTh[:, c:c + 4, t * P:(t + 1) * P].bitcast(FP32), ALU.subtract).then_inc(W.xT_split, 1)

                def duty(n):
                    kind, j = PIECES[layer][n]
                    b = j % 2
                    f = product_after(layer, n)
                    if f is not None:
                        dve.wait_ge(B.yh_ready, f + 1)
                        nc.vector.tensor_tensor(yTl[:, f % 2, :], y[:, f % 2, :], yTh[:, f % 2, :].bitcast(FP32),
                                                ALU.subtract).then_inc(B.yl_ready, 1)
                        if f % 6 == 1 and f < 18:
                            normalise_v(f // 6 + 1)
                    if kind == "X":
                        dve.wait_ge(W.c_copied, j + 1)
                        step(nc.vector.tensor_tensor(padded[:, b, 2:T + 2], c_gate[:, b, :], ps[:, 2 * b, T:2 * T], ALU.mult))
                        step(nc.vector.tensor_scalar(conv[:], padded[:, b, 2:T + 2], conv_w[:, j, 2:3], None, ALU.mult))
                        for tap in (1, 0):
                            step(nc.vector.scalar_tensor_tensor(conv[:], padded[:, b, tap:T + tap], conv_w[:, j, tap:tap + 1],
                                                                conv[:], ALU.mult, ALU.add))
                    elif kind == "B":
                        nc.vector.tensor_tensor(aT[:, b, :], conv[:], ps[:, 2 * b + 1, 0:T], ALU.mult).then_inc(W.a_ready, 1)
                    elif kind == "C" and j or kind == "out" and j == 0 and layer == 0:
                        dt = j - 1 if kind == "C" else KC - 1
                        dve.wait_ge(W.ah_ready, dt + 1)
                        nc.vector.tensor_tensor(al[:, dt, :], aT[:, dt % 2, :], ah[:, dt, :].bitcast(FP32),
                                                ALU.subtract).then_inc(W.al_ready, 1)
                    elif kind == "v" and j % KC == KC - 1:
                        for m in range(4):
                            t, nh = m // 2, m % 2
                            dve.wait_ge(B.v_gelu, 4 * (j // KC) + m + 1)
                            lo = (j // KC) * 768 + nh * 384
                            last = nc.vector.bn_stats(stats[:, t, 2 * (j // KC) + nh, :], v[:, t, lo:lo + 384])
                        if j == 4 * KC - 1:
                            step(last)
                            for t in range(TT):
                                moments(t, 8, B.v_var)
                            normalise_v(0)
                            dve.wait_ge(B.sums_ready, 2)
                            dve.wait_ge(g.gb_in, 16)
                    if kind == "u":
                        head = j // TILES_PER_HEAD
                        step(nc.vector.scalar_tensor_tensor(s_off[:, b, :], ws_sum[:, head, :], b_gb[:, 1, j:j + 1],
                                                            s_bias[:, head, :], ALU.mult, ALU.add))
                        dve.wait_ge(B.spatial, j + 1)
                        step(nc.vector.scalar_tensor_tensor(
                            s_val[:, b, :].rearrange("p (t q) -> p t q", t=TT),
                            ps[:, 2 + b, 0:T].rearrange("p (t q) -> p t q", t=TT), b_gb[:, 0, j:j + 1],
                            s_off[:, b, :].unsqueeze(1).to_broadcast([P, TT, P]), ALU.mult, ALU.add))
                        dve.wait_ge(B.u_gelu, j + 1)
                        nc.vector.tensor_tensor(y[:, b, :], s_val[:, b, :], uT[:, b, :], ALU.mult).then_inc(B.y_ready, 1)

                def normalise_v(j):
                    for t in range(TT):
                        dve.wait_ge(B.v_rstd, t + 1)
                        cols = slice(j * 768, (j + 1) * 768)
                        nc.vector.tensor_scalar(v[:, t, cols], v[:, t, cols], mv[:, t, 0:1], rstd[:, t:t + 1],
                                                ALU.subtract, ALU.mult).then_inc(B.v_norm, 1)

                for n in range(len(PIECES[layer]) + 1):
                    if n < len(PIECES[layer]) and not (layer and n == 0):
                        split_low(layer, n)
                    if n >= BEHIND:
                        dve.wait_ge(W.used, n - BEHIND + 1)
                        duty(n - BEHIND)
                dve.wait_ge(g.x_in, 16)
                dve.wait_ge(g.small, 32)

                def residual(t):
                    dve.wait_ge(W.out_done, t + 1)
                    step(nc.vector.scalar_tensor_tensor(
                        acc[:, t, :], x_tok[:, t, :], ALPHA,
                        ps[:, 4 + 2 * t:6 + 2 * t, :].rearrange("p a b -> p (a b)"), ALU.mult, ALU.add))

                layer_norm(W.ln_rows, W.ln_var, W.ln_rstd, W.x_ready, 0, 2, residual)
                def low_of_x(t):
                    dve.wait_ge(W.xh_ready, t + 1)
                    nc.vector.tensor_tensor(xl[:, t], x_tok[:, t, :].rearrange("p (q c) -> p c q", c=KC),
                                            xh[:, t].bitcast(FP32), ALU.subtract).then_inc(W.xl_ready, 1)

                low_of_x(0)
                dve.wait_ge(W.scored, 1)
                step(nc.vector.tensor_tensor(biased[:], score[:], rb[:, layer, :].unsqueeze(1).to_broadcast([P, TT, E]), ALU.add))
                for t in range(TT):
                    for j in range(GROUPS):
                        last = nc.vector.max(top8[:, t, j, :], biased[:, t, j * PER_GROUP:(j + 1) * PER_GROUP])
                step(last)
                step(nc.vector.tensor_tensor(g_score[:], top8[:, :, :, 0], top8[:, :, :, 1], ALU.add))
                other, own = (g_score[:].unsqueeze(2).to_broadcast([P, TT, GROUPS, GROUPS]),
                              g_score[:].unsqueeze(3).to_broadcast([P, TT, GROUPS, GROUPS]))
                step(nc.vector.tensor_tensor(g_more[:], other, own, ALU.is_gt))
                step(nc.vector.tensor_tensor(g_tied[:], other, own, ALU.is_equal))
                step(nc.vector.tensor_tensor(g_tied[:], g_tied[:], tri[:].unsqueeze(1).to_broadcast([P, TT, GROUPS, GROUPS]), ALU.mult))
                step(nc.vector.tensor_tensor(g_more[:], g_more[:], g_tied[:], ALU.add))
                step(nc.vector.reduce_sum(g_rank[:], g_more[:], AX.X))
                step(nc.vector.tensor_scalar(g_rank[:], g_rank[:], TOPK_GROUPS - 0.5, NEG, ALU.is_gt, ALU.mult))
                step(nc.vector.tensor_tensor(
                    masked[:].rearrange("p t (g e) -> p t g e", g=GROUPS), biased[:].rearrange("p t (g e) -> p t g e", g=GROUPS),
                    g_rank[:].unsqueeze(3).to_broadcast([P, TT, GROUPS, PER_GROUP]), ALU.add))
                for t in range(TT):
                    step(nc.vector.max(best[:, t, :], masked[:, t, :]))
                    step(nc.vector.match_replace(marked[:, t, :], best[:, t, :], masked[:, t, :], 4 * NEG))
                nc.vector.tensor_tensor(chosen[:], marked[:], masked[:], ALU.is_lt).then_inc(W.chosen, 1)
                dve.wait_ge(W.chosen, 1)
                step(nc.vector.tensor_tensor(masked[:], score[:], chosen[:], ALU.mult))
                step(nc.vector.reduce_sum(w_sum[:], masked[:], AX.X))
                step(nc.vector.reciprocal(w_inv[:], w_sum[:]))
                for t in range(TT):
                    last = nc.vector.tensor_scalar(gates[:, t, 0:E], masked[:, t, :], w_inv[:, t:t + 1], ROUTED_SCALE,
                                                   ALU.mult, ALU.mult)
                step(last)
                step(nc.vector.tensor_copy(g_cols[:, :, QUAD], own_i[:]))
                low_of_x(1)
                dve.wait_ge(W.ranks, 1)
                step(nc.vector.scalar_tensor_tensor(marked[:], ps[:, 3, 0:TT * E].rearrange("p (t e) -> p t e", t=TT), 1.0,
                                                    chosen[:], ALU.add, ALU.mult))
                step(nc.vector.tensor_scalar(rank[:, :, 0:E], marked[:], -1.0, None, ALU.add))
                k = MAIN[layer]
                select(k, 0)
                step(nc.vector.reduce_max(count[:], ps[:, 3, 2 * E:3 * E], AX.X))
                step(nc.vector.tensor_scalar(over_f[:], count[:], SPAN + 0.5, None, ALU.is_gt))
                nc.vector.tensor_copy(over[:], over_f[0:1, :]).then_inc(W.over, 1)
                nc.vector.memset(w_sum[:, 0:1], 0.0).then_inc(k.comb_taken, 2)

                def shared_hidden():
                    for t in range(TT):
                        dve.wait_ge(W.sh_sig, t + 1)
                        step(nc.vector.tensor_tensor(sgated[:, t, :], ssig[:, t, :], ps[:, SHARED_BANKS[t], 0:H], ALU.mult))
                        nc.vector.tensor_tensor(shid[:, t, :], sgated[:, t, :], ps[:, SHARED_BANKS[t], H:2 * H], ALU.mult).then_inc(W.sh_h, 1)

                shared_hidden()
                experts(k, 0)
                more = dve.value_load(over[0:1, 0:1], min_val=0, max_val=1)
                with dve.If(more > 0):
                    o = OVER[layer]
                    for p in range(1, PASSES):
                        nc.vector.tensor_copy(gates[:, :, p * E:(p + 1) * E], gates[:, :, 0:E])
                        last = nc.vector.tensor_scalar(rank[:, :, p * E:(p + 1) * E], rank[:, :, 0:E], -1.0 * SPAN * p, None, ALU.add)
                    dve.wait_ge(k.comb_taken, k.base.comb_taken + (4 * QUADS + 2))
                    nc.vector.memset(slot_gate[:, 1:2], 0.0).then_inc(o.comb_taken, 2)
                    last.then_inc(W.over_ranks, 1)
                    dve.wait_ge(W.over_ranks, 1)
                    select(o, E)
                    experts(o, E)
                    dve.wait_ge(o.comb_taken, o.base.comb_taken + (4 * QUADS * (PASSES - 1) + 2))
                    dve.wait_ge(o.stats_done, o.base.stats_done + 4)
                    dve.wait_ge(W.over_rows, 2)
                    dve.nop()
                with dve.Else():
                    if layer == 0:
                        dve.wait_ge(W.first_done, 1)
                        skip_experts(dve, OVER[layer], "s_ready info_taken gated h_ready yl_ready c_ready comb_taken stats_done")
                    else:
                        dve.nop()
                dve.wait_ge(k.comb_taken, k.base.comb_taken + (4 * QUADS + 2))
                dve.wait_ge(k.stats_done, k.base.stats_done + 4)
                layer_norm(W.ln2_rows, W.ln2_var, W.ln2_rstd, W.x2_ready, 6, 0)


def kernel(**inputs):
    import concourse.bacc as bacc
    import numpy as np
    from concourse.bass_utils import run_bass_kernel_spmd

    a = {k: np.asarray(v) for k, v in inputs.items()}
    x = np.ascontiguousarray(a["x"][0])
    arrays = {
        "x": x,
        "xT0": np.ascontiguousarray(x.T.reshape(P, KC, T)),
        "a_w_in": a["a_w_in"][0],
        "a_conv_w": np.ascontiguousarray(a["a_conv_w"][0].T.reshape(KC, P, 3).transpose(1, 0, 2)),
        "a_w_out": a["a_w_out"][0],
        "b_w_in": a["b_w_in"][0],
        "b_ln": np.ascontiguousarray(np.stack([a["b_v_ln_g"][0].reshape(GT, P).T, a["b_v_ln_b"][0].reshape(GT, P).T], 1)),
        "b_wsT": np.ascontiguousarray(a["b_w_s"][0].transpose(2, 0, 1)),
        "b_w_out": a["b_w_out"][0],
        "rows": np.stack([a[n][i] for i in range(DEPTH) for n in ("ln1_g", "ln1_b", "ln2_g", "ln2_b")]
                         + [a["b_s_bias"][0].reshape(D)]),
        "router_w": a["router_w"],
        "router_bias": a["router_bias"],
        "w_gate": a["exp_w_gate"],
        "w_up": a["exp_w_up"],
        "w_down": a["exp_w_down"],
        "sh_gate": a["sh_w_gate"],
        "sh_up": a["sh_w_up"],
        "sh_down": a["sh_w_down"],
    }
    nc = bacc.Bacc("TRN2", target_bir_lowering=False, num_devices=1, dynamic_dma_scratch_size=1024)
    feeds, args = {}, []
    for name, value in arrays.items():
        value = np.ascontiguousarray(value)
        feeds[f"in_{name}"] = value
        args.append(nc.dram_tensor(f"in_{name}", value.shape, mybir.dt.from_np(value.dtype), kind="ExternalInput").ap())
    args.append(nc.dram_tensor("out_x", (T, D), FP32, kind="ExternalOutput").ap())
    build(nc, *args)
    result = run_bass_kernel_spmd(nc, [feeds], core_ids=[0])
    return result.results[0]["out_x"].reshape(1, T, D)
```
